# Optimizing a Trainium2 kernel written in Bass

```python
import jax, jax.numpy as jnp
from jax import lax
import numpy as np

D_MODEL = 1024
BATCH = 1
SEQ = 512
DEPTH = 2

HEAD_DIM = 64
N_MEM = 256
MEM_HEADS = 4
CROSS_WIDTH = MEM_HEADS * HEAD_DIM
MIX_WIDTH = 12 * HEAD_DIM
ATTN_WIDTH = MIX_WIDTH + CROSS_WIDTH
EPS = 1e-6
NEG = -1e30
MLA_HEADS = 12
MLA_Q_RANK = 384
MLA_KV_RANK = 256
MLA_NOPE = 64
MLA_ROPE = 32
MLA_V = 64
MLA_QK = MLA_NOPE + MLA_ROPE
ROPE_THETA = 10000.0
Q_BLOCK = 128
MLA_IN = MLA_Q_RANK + MLA_KV_RANK + MLA_ROPE + CROSS_WIDTH
SWA_Q_HEADS = 12
SWA_KV_HEADS = 4
SWA_GROUP = SWA_Q_HEADS // SWA_KV_HEADS
WINDOW = 128
SWA_IN = (SWA_Q_HEADS + 2 * SWA_KV_HEADS) * HEAD_DIM + CROSS_WIDTH
D_FF = 4 * D_MODEL
N_MLA_LAYERS = (DEPTH + 1) // 2
N_SWA_LAYERS = DEPTH // 2


def rmsnorm(x, g):
    xf = x.astype(jnp.float32)
    y = xf * lax.rsqrt(jnp.mean(xf * xf, axis=-1, keepdims=True) + EPS)
    return (y * g.astype(jnp.float32)).astype(x.dtype)

def rope(x, positions):
    r = x.shape[-1]
    half = r // 2
    inv = ROPE_THETA ** (-(jnp.arange(half, dtype=jnp.float32) * 2.0) / r)
    ang = positions.astype(jnp.float32)[..., None] * inv
    cos = jnp.cos(ang)[:, :, None, :]
    sin = jnp.sin(ang)[:, :, None, :]
    xf = x.astype(jnp.float32)
    x1, x2 = xf[..., :half], xf[..., half:]
    out = jnp.concatenate([x1 * cos - x2 * sin, x1 * sin + x2 * cos], axis=-1)
    return out.astype(x.dtype)

def alibi_slopes(n_heads):
    return 2.0 ** (-8.0 * (jnp.arange(n_heads, dtype=jnp.float32) + 1.0) / n_heads)

def causal_dense_attention(q, k, v):
    b, s, h, dk = q.shape
    dv = v.shape[-1]
    nb = s // Q_BLOCK
    scale = dk ** -0.5
    qb = q.reshape(b, nb, Q_BLOCK, h, dk).transpose(1, 0, 2, 3, 4)
    k_idx = jnp.arange(s)

    def one_block(args):
        q_blk, n = args
        t_idx = n * Q_BLOCK + jnp.arange(Q_BLOCK)
        sc = jnp.einsum('bqhd,bkhd->bhqk', q_blk, k,
                        preferred_element_type=jnp.float32) * scale
        mask = k_idx[None, :] <= t_idx[:, None]
        sc = jnp.where(mask[None, None], sc, NEG)
        p = jax.nn.softmax(sc, axis=-1).astype(v.dtype)
        return jnp.einsum('bhqk,bkhd->bqhd', p, v)

    out = lax.map(one_block, (qb, jnp.arange(nb)))
    return out.transpose(1, 0, 2, 3, 4).reshape(b, s, h, dv)

def mla_mixer(hn, positions, w_in, q_norm_g, kv_norm_g, w_uq, w_ukv):
    b, s, _ = hn.shape
    proj = hn @ w_in
    c_q = proj[..., :MLA_Q_RANK]
    c_kv = proj[..., MLA_Q_RANK:MLA_Q_RANK + MLA_KV_RANK]
    k_r = proj[..., MLA_Q_RANK + MLA_KV_RANK:MLA_Q_RANK + MLA_KV_RANK + MLA_ROPE]
    q_cross = proj[..., MLA_Q_RANK + MLA_KV_RANK + MLA_ROPE:]
    q = (rmsnorm(c_q, q_norm_g) @ w_uq).reshape(b, s, MLA_HEADS, MLA_QK)
    q = jnp.concatenate([q[..., :MLA_NOPE], rope(q[..., MLA_NOPE:], positions)], axis=-1)
    kv = (rmsnorm(c_kv, kv_norm_g) @ w_ukv).reshape(b, s, MLA_HEADS, MLA_NOPE + MLA_V)
    k_nope, v = kv[..., :MLA_NOPE], kv[..., MLA_NOPE:]
    k_rope = jnp.broadcast_to(rope(k_r[:, :, None, :], positions),
                              (b, s, MLA_HEADS, MLA_ROPE))
    k = jnp.concatenate([k_nope, k_rope], axis=-1)
    o = causal_dense_attention(q, k, v)
    return o.reshape(b, s, MLA_HEADS * MLA_V), q_cross

def _with_prev_block(a):
    pad = [(0, 0), (1, 0)] + [(0, 0)] * (a.ndim - 2)
    prev = jnp.pad(a[:, :-1], pad)
    return jnp.concatenate([prev, a], axis=2)

def swa_mixer(hn, positions, w_in, sinks):
    b, s, _ = hn.shape
    nb = s // WINDOW
    proj = hn @ w_in
    nq = SWA_Q_HEADS * HEAD_DIM
    nk = SWA_KV_HEADS * HEAD_DIM
    q = proj[..., :nq].reshape(b, nb, WINDOW, SWA_KV_HEADS, SWA_GROUP, HEAD_DIM)
    k = proj[..., nq:nq + nk].reshape(b, nb, WINDOW, SWA_KV_HEADS, HEAD_DIM)
    v = proj[..., nq + nk:nq + 2 * nk].reshape(b, nb, WINDOW, SWA_KV_HEADS, HEAD_DIM)
    q_cross = proj[..., nq + 2 * nk:]
    kk = _with_prev_block(k)
    vv = _with_prev_block(v)
    pos_q = positions.reshape(b, nb, WINDOW)
    pos_k = _with_prev_block(pos_q)
    sc = jnp.einsum('bnqhgd,bnkhd->bnhgqk', q, kk,
                    preferred_element_type=jnp.float32) * (HEAD_DIM ** -0.5)
    dist = (pos_q[..., :, None] - pos_k[..., None, :]).astype(jnp.float32)
    slopes = alibi_slopes(SWA_Q_HEADS).reshape(SWA_KV_HEADS, SWA_GROUP)
    sc = sc - slopes[None, None, :, :, None, None] * dist[:, :, None, None]
    qi = jnp.arange(WINDOW)[:, None]
    kj = jnp.arange(2 * WINDOW)[None, :]
    rel = WINDOW + qi - kj
    band = (rel >= 0) & (rel < WINDOW)
    valid = band[None] & ((jnp.arange(nb)[:, None, None] > 0) | (kj >= WINDOW)[None])
    sc = jnp.where(valid[None, :, None, None], sc, NEG)
    sink = sinks.astype(jnp.float32).reshape(SWA_KV_HEADS, SWA_GROUP)[None, None, :, :, None, None]
    sink = jnp.broadcast_to(sink, sc.shape[:-1] + (1,))
    p = jax.nn.softmax(jnp.concatenate([sc, sink], axis=-1), axis=-1)[..., :-1]
    o = jnp.einsum('bnhgqk,bnkhd->bnqhgd', p.astype(vv.dtype), vv)
    return o.reshape(b, s, SWA_Q_HEADS * HEAD_DIM), q_cross

def memory_cross_attention(q_cross, mem_n, w_mem_kv):
    b, s, _ = q_cross.shape
    kv = (mem_n @ w_mem_kv).reshape(b, N_MEM, 2, MEM_HEADS, HEAD_DIM)
    k, v = kv[:, :, 0], kv[:, :, 1]
    q = q_cross.reshape(b, s, MEM_HEADS, HEAD_DIM)
    sc = jnp.einsum('bshd,bmhd->bhsm', q, k,
                    preferred_element_type=jnp.float32) * (HEAD_DIM ** -0.5)
    p = jax.nn.softmax(sc, axis=-1).astype(v.dtype)
    return jnp.einsum('bhsm,bmhd->bshd', p, v).reshape(b, s, CROSS_WIDTH)

def squared_relu_mlp(h, w_up, w_down):
    a = jax.nn.relu(h @ w_up)
    return (a * a) @ w_down

def first_inputs(seed: int = 0) -> dict:
    key = jax.random.key(seed)
    ks = jax.random.split(key, 20)

    def w(k, shape, fan_in):
        return jax.random.normal(k, shape, jnp.float32) * (fan_in ** -0.5)

    def gain(k, shape):
        return 1.0 + 0.02 * jax.random.normal(k, shape, jnp.float32)

    x = jax.random.normal(ks[0], (BATCH, SEQ, D_MODEL), jnp.float32)
    mem = jax.random.normal(ks[1], (BATCH, N_MEM, D_MODEL), jnp.float32)
    offsets = jax.random.randint(ks[2], (BATCH, 1), 0, 1024, dtype=jnp.int32)
    positions = (offsets + jnp.arange(SEQ, dtype=jnp.int32)[None, :]).astype(jnp.int32)
    return {
        "x": x,
        "mem": mem,
        "positions": positions,
        "attn_norm_g": gain(ks[3], (DEPTH, D_MODEL)),
        "mlp_norm_g": gain(ks[4], (DEPTH, D_MODEL)),
        "mem_norm_g": gain(ks[5], (D_MODEL,)),
        "final_norm_g": gain(ks[6], (D_MODEL,)),
        "mla_w_in": w(ks[7], (N_MLA_LAYERS, D_MODEL, MLA_IN), D_MODEL),
        "mla_q_norm_g": gain(ks[8], (N_MLA_LAYERS, MLA_Q_RANK)),
        "mla_kv_norm_g": gain(ks[9], (N_MLA_LAYERS, MLA_KV_RANK)),
        "mla_w_uq": w(ks[10], (N_MLA_LAYERS, MLA_Q_RANK, MLA_HEADS * MLA_QK), MLA_Q_RANK),
        "mla_w_ukv": w(ks[11], (N_MLA_LAYERS, MLA_KV_RANK, MLA_HEADS * (MLA_NOPE + MLA_V)), MLA_KV_RANK),
        "swa_w_in": w(ks[12], (N_SWA_LAYERS, D_MODEL, SWA_IN), D_MODEL),
        "swa_sinks": 0.5 * jax.random.normal(ks[13], (N_SWA_LAYERS, SWA_Q_HEADS), jnp.float32),
        "w_mem_kv": w(ks[14], (DEPTH, D_MODEL, 2 * CROSS_WIDTH), D_MODEL),
        "w_o": w(ks[15], (DEPTH, ATTN_WIDTH, D_MODEL), ATTN_WIDTH),
        "mlp_w_up": w(ks[16], (DEPTH, D_MODEL, D_FF), D_MODEL),
        "mlp_w_down": w(ks[17], (DEPTH, D_FF, D_MODEL), D_FF),
    }

def first_block(x, mem, positions, attn_norm_g, mlp_norm_g, mem_norm_g, final_norm_g,
              mla_w_in, mla_q_norm_g, mla_kv_norm_g, mla_w_uq, mla_w_ukv,
              swa_w_in, swa_sinks, w_mem_kv, w_o, mlp_w_up, mlp_w_down):
    mem_n = rmsnorm(mem, mem_norm_g)
    for i in range(DEPTH):
        j = i // 2
        hn = rmsnorm(x, attn_norm_g[i])
        if i % 2 == 0:
            mix, q_cross = mla_mixer(hn, positions, mla_w_in[j], mla_q_norm_g[j],
                                     mla_kv_norm_g[j], mla_w_uq[j], mla_w_ukv[j])
        else:
            mix, q_cross = swa_mixer(hn, positions, swa_w_in[j], swa_sinks[j])
        cross = memory_cross_attention(q_cross, mem_n, w_mem_kv[i])
        x = x + jnp.concatenate([mix, cross], axis=-1) @ w_o[i]
        x = x + squared_relu_mlp(rmsnorm(x, mlp_norm_g[i]), mlp_w_up[i], mlp_w_down[i])
    return rmsnorm(x, final_norm_g)


DEPTH_2 = 1

CONV_WIDTH_A = D_MODEL // 2
CONV_K = 3
N_HEADS = 8
N_KV_GROUPS = 2
HEADS_PER_GROUP = N_HEADS // N_KV_GROUPS
ATTN_WIDTH_2 = N_HEADS * HEAD_DIM
KV_WIDTH = N_KV_GROUPS * HEAD_DIM
CMP_BLOCK = 32
CMP_STRIDE = 16
SEL_BLOCK = 64
N_SEL = 16
WINDOW_2 = 512
N_NSA_BRANCH = 3
D_FF_2 = 2816
N_MERGE = 2
NEG_2 = -1e30
FORCE = 1e9

SPLIT_SIZES = [CONV_WIDTH_A, CONV_WIDTH_A, CONV_WIDTH_A, ATTN_WIDTH_2] + [KV_WIDTH] * 6 + [N_NSA_BRANCH * N_HEADS, N_MERGE * D_MODEL]
IN_COLS = sum(SPLIT_SIZES)


def rmsnorm_2(x, g):
    x32 = x.astype(jnp.float32)
    y = x32 * lax.rsqrt(jnp.mean(x32 * x32, axis=-1, keepdims=True) + EPS)
    return (y * g.astype(jnp.float32)).astype(x.dtype)

def causal_dwconv(u, w):
    s = u.shape[1]
    up = jnp.pad(u, ((0, 0), (CONV_K - 1, 0), (0, 0)))
    y = w[0] * up[:, 0:s]
    for k in range(1, CONV_K):
        y = y + w[k] * up[:, k:k + s]
    return y

def rope_2(x, positions):
    half = HEAD_DIM // 2
    inv = ROPE_THETA ** (-jnp.arange(half, dtype=jnp.float32) / half)
    ang = positions.astype(jnp.float32)[..., None] * inv
    cos = jnp.cos(ang)[:, :, None, :]
    sin = jnp.sin(ang)[:, :, None, :]
    x32 = x.astype(jnp.float32)
    x1, x2 = x32[..., :half], x32[..., half:]
    out = jnp.concatenate([x1 * cos - x2 * sin, x2 * cos + x1 * sin], axis=-1)
    return out.astype(x.dtype)

def compress(kv, pe, w1, w2):
    b, s = kv.shape[0], kv.shape[1]
    n_cmp = (s - CMP_BLOCK) // CMP_STRIDE + 1
    idx = np.arange(n_cmp)[:, None] * CMP_STRIDE + np.arange(CMP_BLOCK)[None, :]
    blk = kv[:, idx] + pe[None, None, :, None, :]
    blk = blk.transpose(0, 1, 3, 2, 4).reshape(b, n_cmp, N_KV_GROUPS, CMP_BLOCK * HEAD_DIM)
    return jax.nn.silu(blk @ w1) @ w2

def masked_softmax(s, mask):
    p = jax.nn.softmax(jnp.where(mask, s, NEG_2), axis=-1)
    return jnp.where(mask, p, 0.0)

def nsa(q, k_cmp, v_cmp, k_sel, v_sel, k_win, v_win, gates):
    b, s = q.shape[0], q.shape[1]
    n_cmp = k_cmp.shape[1]
    n_blk = s // SEL_BLOCK
    n_sel = min(N_SEL, n_blk)
    n_qb = s // Q_BLOCK
    scale = HEAD_DIM ** -0.5
    cmp_end = jnp.arange(n_cmp) * CMP_STRIDE + CMP_BLOCK - 1
    ii = np.arange(n_cmp)[:, None] * CMP_STRIDE
    jj = np.arange(n_blk)[None, :] * SEL_BLOCK
    overlap = jnp.asarray(((ii < jj + SEL_BLOCK) & (ii + CMP_BLOCK > jj)).astype(np.float32))
    ksb = k_sel.reshape(b, n_blk, SEL_BLOCK, N_KV_GROUPS, HEAD_DIM).transpose(0, 3, 1, 2, 4)
    vsb = v_sel.reshape(b, n_blk, SEL_BLOCK, N_KV_GROUPS, HEAD_DIM).transpose(0, 3, 1, 2, 4)
    kwp = jnp.pad(k_win, ((0, 0), (WINDOW_2, 0), (0, 0), (0, 0)))
    vwp = jnp.pad(v_win, ((0, 0), (WINDOW_2, 0), (0, 0), (0, 0)))
    b_ix = jnp.arange(b)[:, None, None, None]
    g_ix = jnp.arange(N_KV_GROUPS)[None, :, None, None]
    blk_ids = jnp.arange(n_blk)

    def query_block(qb):
        t0 = qb * Q_BLOCK
        t = t0 + jnp.arange(Q_BLOCK)
        qc = lax.dynamic_slice_in_dim(q, t0, Q_BLOCK, axis=1).reshape(b, Q_BLOCK, N_KV_GROUPS, HEADS_PER_GROUP, HEAD_DIM)
        gc = lax.dynamic_slice_in_dim(gates, t0, Q_BLOCK, axis=1).reshape(b, Q_BLOCK, N_KV_GROUPS, HEADS_PER_GROUP, N_NSA_BRANCH)
        sc = jnp.einsum('bqghd,bkgd->bghqk', qc, k_cmp).astype(jnp.float32) * scale
        p_c = masked_softmax(sc, cmp_end[None, :] <= t[:, None])
        o_c = jnp.einsum('bghqk,bkgd->bqghd', p_c.astype(v_cmp.dtype), v_cmp)
        imp = jnp.einsum('bghqk,kj->bgqj', p_c, overlap)
        cur = t // SEL_BLOCK
        forced = (blk_ids[None, :] == 0) | (blk_ids[None, :] == cur[:, None]) | (blk_ids[None, :] == cur[:, None] - 1)
        valid = blk_ids[None, :] <= cur[:, None]
        imp = jnp.where(forced, FORCE, jnp.where(valid, imp, -FORCE))
        _, sel = lax.top_k(imp, n_sel)
        ks = ksb[b_ix, g_ix, sel].reshape(b, N_KV_GROUPS, Q_BLOCK, n_sel * SEL_BLOCK, HEAD_DIM)
        vs = vsb[b_ix, g_ix, sel].reshape(b, N_KV_GROUPS, Q_BLOCK, n_sel * SEL_BLOCK, HEAD_DIM)
        kpos = (sel[..., None] * SEL_BLOCK + jnp.arange(SEL_BLOCK)).reshape(b, N_KV_GROUPS, Q_BLOCK, n_sel * SEL_BLOCK)
        ss = jnp.einsum('bqghd,bgqkd->bghqk', qc, ks).astype(jnp.float32) * scale
        p_s = masked_softmax(ss, (kpos <= t[None, None, :, None])[:, :, None])
        o_s = jnp.einsum('bghqk,bgqkd->bqghd', p_s.astype(vs.dtype), vs)
        kw = lax.dynamic_slice_in_dim(kwp, t0, WINDOW_2 + Q_BLOCK, axis=1)
        vw = lax.dynamic_slice_in_dim(vwp, t0, WINDOW_2 + Q_BLOCK, axis=1)
        spos = t0 - WINDOW_2 + jnp.arange(WINDOW_2 + Q_BLOCK)
        diff = t[:, None] - spos[None, :]
        mask_w = (diff >= 0) & (diff < WINDOW_2) & (spos[None, :] >= 0)
        sw = jnp.einsum('bqghd,bkgd->bghqk', qc, kw).astype(jnp.float32) * scale
        p_w = masked_softmax(sw, mask_w)
        o_w = jnp.einsum('bghqk,bkgd->bqghd', p_w.astype(vw.dtype), vw)
        out = gc[..., 0:1] * o_c + gc[..., 1:2] * o_s + gc[..., 2:3] * o_w
        return out.reshape(b, Q_BLOCK, ATTN_WIDTH_2)

    out = lax.map(query_block, jnp.arange(n_qb))
    return out.transpose(1, 0, 2, 3).reshape(b, s, ATTN_WIDTH_2)

def second_inputs(seed: int = 0) -> dict:
    key = jax.random.key(seed)
    ks = jax.random.split(key, 24)
    L = DEPTH_2
    nrm = lambda k, shape, scale: jax.random.normal(k, shape, jnp.float32) * scale
    x = jax.random.normal(ks[0], (BATCH, SEQ, D_MODEL), jnp.float32)
    positions = (jnp.arange(SEQ, dtype=jnp.int32)[None, :] + jax.random.randint(ks[1], (BATCH, 1), 0, 1024, dtype=jnp.int32)).astype(jnp.int32)
    return {
        'x': x,
        'positions': positions,
        'norm1_g': 1.0 + nrm(ks[2], (L, D_MODEL), 0.02),
        'w_in': nrm(ks[3], (L, D_MODEL, IN_COLS), D_MODEL ** -0.5),
        'conv_a_w': nrm(ks[4], (L, CONV_K, CONV_WIDTH_A), CONV_K ** -0.5),
        'w_a_out': nrm(ks[5], (L, CONV_WIDTH_A, D_MODEL), CONV_WIDTH_A ** -0.5),
        'q_norm_g': 1.0 + nrm(ks[6], (L, HEAD_DIM), 0.02),
        'k_norm_g': 1.0 + nrm(ks[7], (L, N_NSA_BRANCH, HEAD_DIM), 0.02),
        'cmp_k_pe': nrm(ks[8], (L, CMP_BLOCK, HEAD_DIM), 0.1),
        'cmp_k_w1': nrm(ks[9], (L, CMP_BLOCK * HEAD_DIM, HEAD_DIM), (CMP_BLOCK * HEAD_DIM) ** -0.5),
        'cmp_k_w2': nrm(ks[10], (L, HEAD_DIM, HEAD_DIM), HEAD_DIM ** -0.5),
        'cmp_v_pe': nrm(ks[11], (L, CMP_BLOCK, HEAD_DIM), 0.1),
        'cmp_v_w1': nrm(ks[12], (L, CMP_BLOCK * HEAD_DIM, HEAD_DIM), (CMP_BLOCK * HEAD_DIM) ** -0.5),
        'cmp_v_w2': nrm(ks[13], (L, HEAD_DIM, HEAD_DIM), HEAD_DIM ** -0.5),
        'w_b_out': nrm(ks[14], (L, ATTN_WIDTH_2, D_MODEL), ATTN_WIDTH_2 ** -0.5),
        'w_o': nrm(ks[15], (L, D_MODEL, D_MODEL), D_MODEL ** -0.5),
        'norm2_g': 1.0 + nrm(ks[16], (L, D_MODEL), 0.02),
        'w_ffn_in': nrm(ks[17], (L, D_MODEL, 2 * D_FF_2), D_MODEL ** -0.5),
        'ffn_conv_w': nrm(ks[18], (L, CONV_K, D_FF_2), CONV_K ** -0.5),
        'ffn_conv_b': nrm(ks[19], (L, D_FF_2), 0.02),
        'w_ffn_out': nrm(ks[20], (L, D_FF_2, D_MODEL), D_FF_2 ** -0.5),
    }

def second_block(x, positions, norm1_g, w_in, conv_a_w, w_a_out, q_norm_g, k_norm_g, cmp_k_pe, cmp_k_w1, cmp_k_w2, cmp_v_pe, cmp_v_w1, cmp_v_w2, w_b_out, w_o, norm2_g, w_ffn_in, ffn_conv_w, ffn_conv_b, w_ffn_out):
    b, s, _ = x.shape
    cuts = list(np.cumsum(SPLIT_SIZES)[:-1].tolist())
    for l in range(DEPTH_2):
        h = rmsnorm_2(x, norm1_g[l])
        proj = h @ w_in[l]
        a_b, a_c, a_x, q, kc, vc, ksl, vsl, kwn, vwn, g_nsa, g_merge = jnp.split(proj, cuts, axis=-1)
        y_a = a_b * causal_dwconv(a_c * a_x, conv_a_w[l])
        q = rope_2(rmsnorm_2(q.reshape(b, s, N_HEADS, HEAD_DIM), q_norm_g[l]), positions)
        kv_shape = (b, s, N_KV_GROUPS, HEAD_DIM)
        k_cmp = rmsnorm_2(compress(kc.reshape(kv_shape), cmp_k_pe[l], cmp_k_w1[l], cmp_k_w2[l]), k_norm_g[l, 0])
        v_cmp = compress(vc.reshape(kv_shape), cmp_v_pe[l], cmp_v_w1[l], cmp_v_w2[l])
        k_sel = rope_2(rmsnorm_2(ksl.reshape(kv_shape), k_norm_g[l, 1]), positions)
        k_win = rope_2(rmsnorm_2(kwn.reshape(kv_shape), k_norm_g[l, 2]), positions)
        gates = jax.nn.sigmoid(g_nsa).reshape(b, s, N_HEADS, N_NSA_BRANCH)
        y_b = nsa(q, k_cmp, v_cmp, k_sel, vsl.reshape(kv_shape), k_win, vwn.reshape(kv_shape), gates)
        gm = jax.nn.sigmoid(g_merge)
        mix = gm[..., :D_MODEL] * (y_a @ w_a_out[l]) + gm[..., D_MODEL:] * (y_b @ w_b_out[l])
        x = x + mix @ w_o[l]
        h = rmsnorm_2(x, norm2_g[l])
        gu = h @ w_ffn_in[l]
        g = causal_dwconv(gu[..., :D_FF_2], ffn_conv_w[l]) + ffn_conv_b[l]
        x = x + (jax.nn.silu(g) * gu[..., D_FF_2:]) @ w_ffn_out[l]
    return x


def setup_inputs(seed=0):
    out = dict(first_inputs(seed))
    for name, value in second_inputs(seed + 1).items():
        if name != "x":
            out[name + "_2"] = value
    return out


def reference(
    x, mem, positions, attn_norm_g, mlp_norm_g, mem_norm_g, final_norm_g, mla_w_in,
    mla_q_norm_g, mla_kv_norm_g, mla_w_uq, mla_w_ukv, swa_w_in, swa_sinks, w_mem_kv, w_o,
    mlp_w_up, mlp_w_down, positions_2, norm1_g_2, w_in_2, conv_a_w_2, w_a_out_2, q_norm_g_2,
    k_norm_g_2, cmp_k_pe_2, cmp_k_w1_2, cmp_k_w2_2, cmp_v_pe_2, cmp_v_w1_2, cmp_v_w2_2,
    w_b_out_2, w_o_2, norm2_g_2, w_ffn_in_2, ffn_conv_w_2, ffn_conv_b_2, w_ffn_out_2,
):
    x = first_block(
        x, mem, positions, attn_norm_g, mlp_norm_g, mem_norm_g, final_norm_g, mla_w_in,
        mla_q_norm_g, mla_kv_norm_g, mla_w_uq, mla_w_ukv, swa_w_in, swa_sinks, w_mem_kv, w_o,
        mlp_w_up, mlp_w_down,
    )
    return second_block(
        x, positions_2, norm1_g_2, w_in_2, conv_a_w_2, w_a_out_2, q_norm_g_2, k_norm_g_2,
        cmp_k_pe_2, cmp_k_w1_2, cmp_k_w2_2, cmp_v_pe_2, cmp_v_w1_2, cmp_v_w2_2, w_b_out_2,
        w_o_2, norm2_g_2, w_ffn_in_2, ffn_conv_w_2, ffn_conv_b_2, w_ffn_out_2,
    )


_drawn_inputs = setup_inputs


def setup_inputs(seed=0):
    import zlib

    import numpy as np

    out = dict(_drawn_inputs(seed))
    spreads = {}
    factors = {'attn_norm_g': 5.722,
     'mem_norm_g': 8.0,
     'mla_q_norm_g': 8.0,
     'mla_kv_norm_g': 8.0,
     'swa_sinks': 21.64,
     'norm1_g_2': 3.039,
     'q_norm_g_2': 31.841,
     'k_norm_g_2': 32.543,
     'cmp_k_pe_2': 23.021,
     'cmp_v_pe_2': 31.632,
     'norm2_g_2': 14.154,
     'ffn_conv_b_2': 20.921}
    for name, (base, spread) in spreads.items():
        noise = np.random.default_rng([zlib.crc32(name.encode()), seed]).standard_normal(out[name].shape)
        drawn = base * np.exp(spread * noise) if base else spread * noise
        out[name] = __import__('jax').numpy.asarray(drawn.astype(out[name].dtype))
    for name, factor in factors.items():
        out[name] = (out[name] * factor).astype(out[name].dtype)
    return out
```

```python
from contextlib import ExitStack

import numpy as np

import concourse.bass as bass
from concourse import mybir

F32 = mybir.dt.float32
F32R = mybir.dt.float32r
I32 = mybir.dt.int32
ALU = mybir.AluOpType
ACT = mybir.ActivationFunctionType
AXX = mybir.AxisListType.X

P = 128
S = 512
NT = S // P
D = 1024
KD = D // P
NMEM = 256
EPS = 1e-6
NEG = -1e30
HD = 64
NH = 12
MH = 4
ROPE = 32
QK = HD + ROPE
KQ, KKV = 3, 2
NKV = 4
NH2 = 8
NG = 2
CMP = 32
NCMP = (S - CMP) // (CMP // 2) + 1
CH = 8
NCH = 4
FF2 = 22
FF2P = 24
RING = 4
AHEAD = 3
TURN_LAG, VALUE_LAG = 3, 5
UPT = 8
TW = UPT * P
MAGIC = float(1.5 * 2 ** 23)
TWO_PI_1 = 6.28125
TWO_PI_2 = round((2 * np.pi - TWO_PI_1) * 2 ** 20) / 2 ** 20
TWO_PI_PARTS = [TWO_PI_1, TWO_PI_2, 2 * np.pi - TWO_PI_1 - TWO_PI_2]
PI_MAX = 3.1415925
SCALE = HD ** -0.5
MLA_SCALE = QK ** -0.5


def columns(sizes):
    at, out = 0, {}
    for name, n in sizes:
        out[name] = at
        at += n
    return out, at


CONST, NCONST = columns([
    ("tri", S), ("ident", P), ("ones", P), ("rot96", P), ("head_ones", P), ("rot128", P),
    ("band", 2 * P), ("cmp_mask", NT * 32), ("cmp_valid", NT), ("slopes", NH), ("inv_mla", 1), ("inv_nsa", 1)])

GAIN, NGAIN = columns([
    ("attn0", KD), ("attn1", KD), ("mlp0", KD), ("mlp1", KD), ("mem", KD), ("final", KD), ("c_kv", KKV),
    ("c_q", KQ), ("norm1", KD), ("norm2", KD), ("q", 1), ("k_cmp", 1), ("k_sel", 1), ("k_win", 1),
    ("conv_a", 3 * 4), ("ffn_conv", 3 * FF2), ("ffn_b", FF2), ("sinks", NH), ("pe_k", 16), ("pe_v", 16)])


class Plan:

    def __init__(self):
        self.steps, self.tile0, self.out0 = {}, {}, {}
        self.tiles = self.outs = 0

    def stage(self, name, tiles, outs, steps):
        self.tile0[name], self.out0[name] = self.tiles, self.outs
        self.steps[name] = [(self.tiles + t, c, w, k, self.outs + o) for t, c, w, k, o in steps]
        self.tiles += tiles
        self.outs += outs

    def count_marks(self):
        every = [s for steps in self.steps.values() for s in steps]
        last_tile, last_out, first_out = {}, {}, {}
        for i, (t, _, _, _, o) in enumerate(every):
            last_tile[t], last_out[o] = i, i
            first_out.setdefault(o, i)
        marks = sorted(set(last_tile.values()) | set(last_out.values()))
        count = {i: n + 1 for n, i in enumerate(marks)}
        self.tile_mark = {t: count[i] for t, i in last_tile.items()}
        self.out_mark = {o: count[i] for o, i in last_out.items()}
        self.out_tile = {o: every[i][0] for o, i in last_out.items()}
        at = 0
        for name, steps in self.steps.items():
            self.steps[name] = [
                s + (at + j in count, first_out[s[4]] == at + j, last_out[s[4]] == at + j)
                for j, s in enumerate(steps)]
            at += len(steps)


def by_output(n_out, n_k, n_kp=None):
    n_kp = n_kp or n_k
    return [((m * n_kp + k) // UPT, (m * n_kp + k) % UPT * P, P, k, m) for m in range(n_out) for k in range(n_k)]


def by_tokens(n_k, width, n_blocks, per_tile):
    return [(k0 // per_tile, (k - k0) * width, width, k, b)
            for k0 in range(0, n_k, per_tile) for b in range(n_blocks) for k in range(k0, k0 + per_tile)]


def shift(steps, tile, out):
    return [(t + tile, c, w, k, o + out) for t, c, w, k, o in steps]


def make_plan():
    p = Plan()
    p.stage("in0", 8, 8, by_output(8, KD))
    mem = []
    for l in range(2):
        mem += shift(by_output(2, KD), 4 * l, 4 * l) + shift(by_tokens(KD, 2 * P, 2, 4), 4 * l + 2, 4 * l + 2)
    p.stage("mem", 8, 8, mem)
    up = by_output(6, KKV)
    up += [(1, 4 * P + k * 256, 256, k, 6 + b) for b in range(NT) for k in range(KKV)]
    up += [(2, k * S, S, k, 10 + b) for b in range(NT) for k in range(KKV)]
    up += [(3 + h // 3, (h % 3 * KQ + k) * QK, QK, k, 14 + h) for h in range(NH) for k in range(KQ)]
    p.stage("up0", 7, 26, up)
    mlp = []
    for c in range(NCH):
        mlp += shift(by_output(CH, KD), 16 * c, 16 * c) + shift(by_output(KD, CH), 16 * c + 8, 16 * c + 8)
    p.stage("wo0", 8, 8, by_output(8, KD))
    p.stage("mlp0", 64, 64, mlp)
    p.stage("in1", 12, 14, by_output(2, KD) + shift(by_tokens(KD, 2 * P, NT, 4), 2, 2) + shift(by_output(8, KD), 4, 6))
    p.stage("wo1", 8, 8, by_output(8, KD))
    p.stage("mlp1", 64, 64, mlp)
    p.stage("in2", 23, 28, by_output(8, KD) + shift(by_tokens(KD, 2 * P, NT, 4), 8, 8)
            + shift(by_tokens(KD, 24, NT, 8), 10, 12) + shift(by_output(12, KD), 11, 16))
    p.stage("merge", 24, 32, [
        s for m in range(KD) for s in
        shift(by_output(2, KD), 3 * m, 4 * m) + shift(by_output(2, 4), 3 * m + 2, 4 * m + 2)])
    p.stage("wo2", 8, 8, by_output(8, KD))
    p.stage("ffn_up", 2 * FF2, 2 * FF2, by_output(2 * FF2, KD))
    p.stage("ffn_down", FF2P, KD, by_output(KD, FF2, FF2P))
    p.count_marks()
    return p


PLAN = make_plan()
NORMS = [("in0", KD), ("mem", KD), ("c_kv", KKV), ("c_q", KQ), ("mlp0", KD), ("in1", KD), ("mlp1", KD),
         ("final", KD), ("norm1", KD), ("norm2", KD)]
NORM_NO = {name: i for i, (name, _) in enumerate(NORMS)}
SQUARES0 = {name: sum(k for _, k in NORMS[:i]) for i, (name, _) in enumerate(NORMS)}
NORM_K = dict(NORMS)


def over(fn, i, n=NCH):
    if isinstance(i, int):
        return fn(i)
    step = fn(1) - fn(0)
    assert all(fn(j) == fn(0) + j * step for j in range(n - 1))
    return i * step + fn(0) if step else fn(0)


class Order:

    def __init__(self, eng, sem):
        self.eng, self.sem, self.n, self.more = eng, sem, 0, 0

    def step(self, ins):
        ins.then_inc(self.sem, 1)
        self.n += 1

    def wait(self):
        self.eng.wait_ge(self.sem, self.more + self.n)

    def then(self, ins):
        self.step(ins)
        self.wait()


class Unit:

    def __init__(self, q, k, nk, mask, scale, values, out_cols, start=True, stop=True, head_end=None,
                 bias=None, sink=None, weight=None):
        self.q, self.k, self.nk, self.mask, self.scale = q, k, nk, mask, scale
        self.values = values
        self.out_cols = out_cols
        self.start, self.stop = start, stop
        self.head_end = head_end
        self.bias, self.sink, self.weight = bias, sink, weight
        self.nb = -(-nk // P)


def program(nc, stream, gains, consts, x, mem, pos_rows, pos_cols, cmp_w1, cmp_w2, out):
    plan = PLAN
    ctx = ExitStack()
    with ctx:
        def tensor(stack, name, shape, dt=F32):
            return stack.enter_context(nc.sbuf_tensor(name, shape, dt))

        X = tensor(ctx, "X", [P, KD, S])
        XH = tensor(ctx, "XH", [P, KD, S], F32R)
        XL = tensor(ctx, "XL", [P, KD, S], F32R)
        RAW = tensor(ctx, "RAW", [P, RING, TW])
        WH = tensor(ctx, "WH", [P, RING, TW], F32R)
        WL = tensor(ctx, "WL", [P, RING, TW], F32R)
        CT = tensor(ctx, "CT", [P, NCONST])
        GV = tensor(ctx, "GV", [P, NGAIN])
        ACC = tensor(ctx, "ACC", [P, S])
        SQ = tensor(ctx, "SQ", [P, S])
        TMP = tensor(ctx, "TMP", [P, 2, S])
        RBC = tensor(ctx, "RBC", [P, S])
        SM = tensor(ctx, "SM", [P, 48])
        POSI = tensor(ctx, "POSI", [P, 2, NT], I32)
        VAR, STD, RCOL, POSQ = SM[:, 0:4], SM[:, 4:8], SM[:, 8:12], SM[:, 12:16]
        MX, NM, SUM, RS = SM[:, 16:20], SM[:, 20:24], SM[:, 24:28], SM[:, 28:32]
        SINK8, CB = SM[:, 32:44], SM[:, 44:46]
        BANK = [ctx.enter_context(nc.psum_tensor(f"bank{i}", [P, S], F32)) for i in range(8)]

        with ExitStack() as block1:
            KM = tensor(block1, "KM", [HD, 2, MH, NMEM])
            VM = tensor(block1, "VM", [P, 2, 2, MH * HD])
            PROB1 = tensor(block1, "PROB1", [P, 3, S])
            PT1 = tensor(block1, "PT1", [P, 2, S])
            QX = tensor(block1, "QX", [HD, MH, S])
            with ExitStack() as mla:
                V0 = tensor(mla, "V0", [P, NT, NH * HD])
                COS0 = tensor(mla, "COS0", [P, S])
                SIN0 = tensor(mla, "SIN0", [P, S])
                with ExitStack() as late:
                    QT0 = tensor(late, "QT0", [QK, NH, S])
                    KT0 = tensor(late, "KT0", [QK, NH, S])
                with ExitStack() as early:
                    C32 = tensor(early, "C32", [P, KKV + KQ, S])
                    KR = tensor(early, "KR", [P, S])
                    POSB0 = tensor(early, "POSB0", [P, S], I32)
                    POSF0 = tensor(early, "POSF0", [P, S])
                    ANG0 = tensor(early, "ANG0", [P, 2, S])
                    MEM = tensor(early, "MEM", [P, KD, NMEM])
                    MH_ = tensor(early, "MH_", [P, KD, NMEM], F32R)
                    ML_ = tensor(early, "ML_", [P, KD, NMEM], F32R)
            with ExitStack() as mlp:
                HH = tensor(mlp, "HH", [P, CH, S], F32R)
                HL = tensor(mlp, "HL", [P, CH, S], F32R)
                RB2 = tensor(mlp, "RB2", [P, S])
                AB = tensor(mlp, "AB", [P, 2, S])
                DT = tensor(mlp, "DT", [P, 2, S])
            with ExitStack() as swa:
                Q1 = tensor(swa, "Q1", [HD, NH, S])
                K1 = tensor(swa, "K1", [HD, NKV, S])
                V1 = tensor(swa, "V1", [P, NT, NKV * HD])
                DIST = tensor(swa, "DIST", [P, NT, 2 * P])
                POSB1 = tensor(swa, "POSB1", [P, S], I32)
                POSF1 = tensor(swa, "POSF1", [P, S])
        with ExitStack() as block2:
            YAH = tensor(block2, "YAH", [P, 4, S], F32R)
            YAL = tensor(block2, "YAL", [P, 4, S], F32R)
            with ExitStack() as before:
                R32 = tensor(before, "R32", [P, 6, S])
                KCS = tensor(before, "KCS", [P, 2, NG, S])
                W1 = tensor(before, "W1", [P, 2, 16, HD])
                W2 = tensor(before, "W2", [HD, 2, HD])
                H1 = tensor(before, "H1", [HD, 2, 64])
                POSB2 = tensor(before, "POSB2", [P, S], I32)
                COS2 = tensor(before, "COS2", [P, S])
                SIN2 = tensor(before, "SIN2", [P, S])
                POSF2 = tensor(before, "POSF2", [P, S])
                UP = tensor(before, "UP", [P, S + 2])
                with ExitStack() as q_k_v:
                    QN = tensor(q_k_v, "QN", [HD, NH2, S])
                    KN = tensor(q_k_v, "KN", [HD, 2, NG, S])
                    VN = tensor(q_k_v, "VN", [P, NT, 2 * P])
                    KC = tensor(q_k_v, "KC", [HD, 64])
                    KCT = tensor(q_k_v, "KCT", [HD, 2, 64])
                    VC = tensor(q_k_v, "VC", [32, P])
                    GATE = tensor(q_k_v, "GATE", [P, NT, 24])
                    PROB2 = tensor(q_k_v, "PROB2", [P, 2, S])
                    PT2 = tensor(q_k_v, "PT2", [P, 2, S])
                with ExitStack() as merged:
                    MIXH = tensor(merged, "MIXH", [P, KD, S], F32R)
                    MIXL = tensor(merged, "MIXL", [P, KD, S], F32R)
            with ExitStack() as after:
                YBH = tensor(after, "YBH", [P, 4, S], F32R)
                YBL = tensor(after, "YBL", [P, 4, S], F32R)
        with ExitStack() as ffn:
            GB = tensor(ffn, "GB", [P, 2, S + 2])
            H2H = tensor(ffn, "H2H", [P, FF2, S], F32R)
            H2L = tensor(ffn, "H2L", [P, FF2, S], F32R)

        signals = {}

        def signal(name):
            if name not in signals:
                signals[name] = ctx.enter_context(nc.semaphore(name))
            return signals[name]

        raw_in = [signal(f"raw_in{j}") for j in range(RING)]
        hi_done, lo_done = signal("hi_done"), signal("lo_done")
        products_done = signal("products_done")
        drained = signal("drained")
        consts_in, x_in, mem_in = signal("consts_in"), signal("x_in"), signal("mem_in")
        squared, added = signal("squared"), signal("added")
        sums_done, std_done = signal("sums_done"), signal("std_done")
        diag_done, scale_done = signal("diag_done"), signal("scale_done")
        scale_used = signal("scale_used")

        def const(name, a=0, n=1):
            return CT[:, CONST[name] + a:CONST[name] + a + n]

        def gain(name, j=0):
            return GV[:, GAIN[name] + j:GAIN[name] + j + 1]

        IDENT, ONES, TRI = const("ident", 0, P), const("ones", 0, P), const("tri", 0, S)

        def blk(t, n=1):
            return slice(t * P, (t + n) * P)

        def cross_units(layer):
            return [Unit(QX[:, h, blk(b)], KM[:, layer, h, :], NMEM, TRI[:, 0:NMEM], SCALE,
                         [VM[:, layer, kb, h * HD:(h + 1) * HD] for kb in range(2)], blk(b),
                         head_end=mix_tile(NH + h) if b == NT - 1 else None)
                    for h in range(MH) for b in range(NT)]

        def mix_tile(h, hi=None, lo=None):
            hi, lo = (XH, XL) if hi is None else (hi, lo)
            rows = slice(HD * (h % 2), HD * (h % 2) + HD)
            return hi[rows, h // 2, :], lo[rows, h // 2, :]

        def mla_units():
            return [Unit(QT0[:, h, blk(b)], KT0[:, h, 0:(b + 1) * P], (b + 1) * P, TRI[:, S - (b + 1) * P:S],
                         MLA_SCALE, [V0[:, kb, h * HD:(h + 1) * HD] for kb in range(b + 1)], blk(b),
                         head_end=mix_tile(h) if b == NT - 1 else None)
                    for h in range(NH) for b in range(NT)] + cross_units(0)

        def swa_units():
            units = []
            for h in range(NH):
                g = h // (NH // NKV)
                for b in range(NT):
                    kb0 = max(b - 1, 0)
                    nk = (b + 1 - kb0) * P
                    units.append(Unit(
                        Q1[:, h, blk(b)], K1[:, g, kb0 * P:kb0 * P + nk], nk, None, SCALE,
                        [V1[:, kb, g * HD:(g + 1) * HD] for kb in range(kb0, b + 1)], blk(b),
                        head_end=mix_tile(h) if b == NT - 1 else None,
                        bias=(DIST[:, b, 2 * P - nk:2 * P], const("slopes", h)), sink=SINK8[:, h:h + 1]))
            return units + cross_units(1)

        def nsa_units():
            units = []
            for h in range(NH2):
                g = h // (NH2 // NG)
                for b in range(NT):
                    def weight(branch):
                        return GATE[:, b, 3 * h + branch:3 * h + branch + 1]
                    units.append(Unit(QN[:, h, blk(b)], KC[:, g * NCMP:(g + 1) * NCMP], NCMP,
                                      const("cmp_mask", b * 32, NCMP), SCALE,
                                      [VC[0:NCMP, g * HD:(g + 1) * HD]], blk(b), stop=False, weight=weight(0)))
                    for br in range(2):
                        units.append(Unit(
                            QN[:, h, blk(b)], KN[:, br, g, 0:(b + 1) * P], (b + 1) * P, TRI[:, S - (b + 1) * P:S],
                            SCALE, [VN[:, kb, br * P + g * HD:br * P + (g + 1) * HD] for kb in range(b + 1)], blk(b),
                            start=False, stop=br == 1, weight=weight(1 + br),
                            head_end=mix_tile(h, YBH, YBL) if b == NT - 1 and br == 1 else None))
            return units

        def ring(*tensors):
            return [t[:, j, :] if len(t.shape) == 3 else t[:] for t in tensors
                    for j in range(t.shape[1] if len(t.shape) == 3 else 1)]

        ATTENTION = {"mla": (mla_units(), ring(PROB1, ACC, SQ), ring(PT1, TMP)),
                     "swa": (swa_units(), ring(PROB1, ACC, SQ), ring(PT1, TMP)),
                     "nsa": (nsa_units(), ring(PROB2, ACC, SQ), ring(PT2, TMP))}
        SCORES, TURNED, HEAD_OUT = (0, 1, 2), (3, 4, 7), (5, 6)
        for units, _, _ in ATTENTION.values():
            h = 0
            for u in units:
                u.head = h
                h += u.head_end is not None

        IN2 = []
        for o in [0, 1, 2, 3, 4, 5, 6, 7, 11, 15] + list(range(16, 28)):
            IN2.append(("out", o))
            after_out = {4: ("norm", 0), 5: ("rotate", 0), 6: ("norm", 1), 7: ("rotate", 1), 11: ("norm", 2),
                         15: ("rotate", 2), 16: ("norm", 3), 17: ("rotate", 3), 18: ("norm", 4),
                         19: ("rotate", 4), 20: ("norm", 5), 21: ("rotate", 5), 22: ("compress", 1),
                         24: ("compress", 2), 26: ("compress", 3)}.get(o)
            if after_out:
                IN2.append(after_out)

        block = ctx.enter_context(nc.Block())

        @block.sync
        def _(sp):
            sp.dma_start(X[:, 0:KD // 2, :], x[:, 0:KD // 2, :]).then_inc(x_in, 16)
            sp.dma_start(X[:, KD // 2:KD, :], x[:, KD // 2:KD, :]).then_inc(x_in, 16)

            def load(n, slot, source):
                if not (isinstance(n, int) and n < RING):
                    sp.wait_ge(lo_done, n - RING + 1)
                sp.dma_start(RAW[:, slot, :], source).then_inc(raw_in[slot], 16)

            for j in range(RING):
                load(j, j, stream[j])
            with sp.Fori(1, plan.tiles // RING) as i:
                for j in range(RING):
                    load(i * RING + j, j, stream[bass.ds(i * RING + j, 1)].rearrange("a p n -> p (a n)"))
            for n in range(plan.tiles // RING * RING, plan.tiles):
                load(n, n % RING, stream[n])
            for m in range(KD):
                sp.wait_ge(drained, plan.out0["ffn_down"] + m + 1)
                sp.dma_start(out[:, m, :], X[:, m, :]).then_inc(signal("out_written"), 16)
            sp.wait_ge(signal("out_written"), 16 * KD)

        @block.gpsimd
        def _(pool):
            def lo_part(n, slot):
                pool.wait_ge(hi_done, n + 1)
                pool.tensor_tensor(WL[:, slot, :], RAW[:, slot, :], WH[:, slot, :].bitcast(F32),
                                   ALU.subtract).then_inc(lo_done, 1)

            with pool.Fori(0, plan.tiles // RING) as i:
                for j in range(RING):
                    lo_part(i * RING + j, j)
            for n in range(plan.tiles // RING * RING, plan.tiles):
                lo_part(n, n % RING)

        @block.tensor
        def _(pe):
            def product(dst, lhs, rhs, start, stop):
                pe.matmul(dst, lhs[0], rhs[0], start=start, stop=False)
                pe.matmul(dst, lhs[0], rhs[1], start=False, stop=False)
                return pe.matmul(dst, lhs[1], rhs[0], start=False, stop=stop)

            def dense(steps_of, i, act, n_tok=S, token_major=(), ready=None, after=None, seen=None):
                seen = set() if seen is None else seen
                tiles_seen = set()
                first = steps_of(0 if not isinstance(i, int) else i)
                o0 = first[0][4]
                for j, (t, c, w, k, o, mark, start, stop) in enumerate(first):
                    if start and o >= RING:
                        pe.wait_ge(drained, over(lambda n: steps_of(n)[j][4] - RING + 1, i, dense.n))
                    if ready and (r := ready(o - o0, k, i)) is not None and r[2] not in seen:
                        seen.add(r[2])
                        pe.wait_ge(r[0], r[1])
                    if t not in tiles_seen:
                        tiles_seen.add(t)
                        pe.wait_ge(lo_done, over(lambda n: steps_of(n)[j][0] + 1, i, dense.n))
                    weights = WH[:, t % RING, c:c + w], WL[:, t % RING, c:c + w]
                    bank = BANK[o % RING]
                    if o - o0 in token_major:
                        tok = token_major[o - o0]
                        ins = product(bank[:, 0:w], [a[:, blk(tok)] for a in act(o - o0, k)], weights, start, stop)
                    else:
                        ins = product(bank[0:w, 0:n_tok], weights, act(o - o0, k), start, stop)
                    if mark:
                        ins.then_inc(products_done, 1)
                    if stop and after and o - o0 in after:
                        for step in after[o - o0]:
                            step()

            dense.n = NCH

            def operand(hi, lo, first=0):
                return lambda o, k: (hi[:, first + k, :], lo[:, first + k, :])

            def sums(norm, tokens=S):
                def step():
                    pe.wait_ge(added, SQUARES0[norm] + NORM_K[norm])
                    for t in range(tokens // P):
                        ins = pe.matmul(BANK[4][:, t:t + 1], ACC[:, blk(t)], ONES[:, 0:1], start=True, stop=True)
                    ins.then_inc(sums_done, 1)
                return step

            def scales(norm, tokens=S):
                def step():
                    n = NORM_NO[norm]
                    if n:
                        pe.wait_ge(scale_used, n)
                    pe.wait_ge(diag_done, n + 1)
                    pe.matmul(BANK[5][:, 0:tokens], ONES, ACC[:, 0:tokens], start=True, stop=True
                              ).then_inc(scale_done, 1)
                return step

            def attention(name, *ready):
                units, prob, pt = ATTENTION[name]
                for sem, value in ready:
                    pe.wait_ge(sem, value)
                n, ns, nt = len(units), len(SCORES), len(TURNED)
                for i in range(n + VALUE_LAG):
                    if i < n:
                        u = units[i]
                        if i >= ns:
                            pe.wait_ge(signal(name + "_biased"), i - ns + 1)
                        pe.matmul(BANK[SCORES[i % ns]][:, 0:u.nk], u.q, u.k, start=True, stop=True
                                  ).then_inc(signal(name + "_scores"), 1)
                    j = i - TURN_LAG
                    if 0 <= j < n:
                        u = units[j]
                        pe.wait_ge(signal(name + "_prob"), j + 1)
                        if j >= nt:
                            pe.wait_ge(signal(name + "_pt"), j - nt + 1)
                        for kb in range(u.nb):
                            w = min(P, u.nk - kb * P)
                            ins = pe.transpose(BANK[TURNED[j % nt]][0:w, blk(kb)],
                                               prob[j % len(prob)][:, kb * P:kb * P + w], IDENT)
                        ins.then_inc(signal(name + "_turned"), 1)
                    j = i - VALUE_LAG
                    if 0 <= j:
                        u = units[j]
                        pe.wait_ge(signal(name + "_pt"), j + 1)
                        if u.head >= 2 and u.start and (j == 0 or units[j - 1].head != u.head):
                            pe.wait_ge(signal(name + "_lo"), u.head - 1)
                        for kb in range(u.nb):
                            w = min(P, u.nk - kb * P)
                            ins = pe.matmul(BANK[HEAD_OUT[u.head % 2]][0:HD, u.out_cols], u.values[kb],
                                            pt[j % len(pt)][0:w, blk(kb)],
                                            start=u.start and kb == 0, stop=u.stop and kb == u.nb - 1)
                        ins.then_inc(signal(name + "_values"), 1)

            def heads_ready(name):
                return lambda o, k, i: (signal(name + "_lo"), 2 * k + 2, k)

            def mlp(name):
                all_steps = plan.steps[name]
                per = len(all_steps) // NCH // 2

                def part(which):
                    return lambda c: all_steps[(2 * c + which) * per:(2 * c + which + 1) * per]

                def chunk(i, seen, after=None):
                    dense(part(0), i, operand(XH, XL), after=after, seen=seen,
                          ready=lambda o, k, _: (signal(name + "_x_lo"), k + 1, k))
                    dense(part(1), i, operand(HH, HL),
                          ready=lambda o, k, _: (signal(name + "_h_lo"),
                                                 over(lambda c: CH * c + k + 1, i), k))

                chunk(0, set(), {0: [sums(name)], 1: [scales(name)]})
                with pe.Fori(1, NCH - 1) as i:
                    chunk(i, set(range(KD)))
                chunk(NCH - 1, set(range(KD)))

            pe.wait_ge(consts_in, 32)
            dense(lambda _: plan.steps["in0"], 0, operand(XH, XL),
                  ready=lambda o, k, i: (signal("in0_x_lo"), k + 1, k),
                  after={0: [sums("in0")], 1: [scales("in0"), sums("mem", NMEM)], 2: [scales("mem", NMEM)],
                         7: [sums("c_kv")]})

            def rotate_key():
                pe.wait_ge(drained, plan.out0["in0"] + 6)
                pe.matmul(BANK[6][HD:QK, :], const("rot96", HD, ROPE)[HD:QK, :], KR[HD:QK, :], start=True, stop=True
                          ).then_inc(signal("key_rotated"), 1)

            dense(lambda _: plan.steps["mem"], 0, operand(MH_, ML_), n_tok=NMEM,
                  token_major={2: 0, 3: 1, 6: 0, 7: 1},
                  ready=lambda o, k, i: (signal("mem_lo"), k + 1, k),
                  after={0: [scales("c_kv")], 1: [sums("c_q")], 3: [scales("c_q"), rotate_key]})

            def rotate_query(h):
                def step():
                    pe.wait_ge(signal("q0_copied"), h + 1)
                    if h >= 2:
                        pe.wait_ge(signal("q0_rotated_read"), h - 1)
                    else:
                        pe.wait_ge(signal("key_placed"), 1)
                    pe.matmul(BANK[6 + h % 2][0:QK, :], const("rot96", 0, QK)[0:QK, :], TMP[0:QK, h % 2, :],
                              start=True, stop=True).then_inc(signal("q0_rotated"), 1)
                return step

            dense(lambda _: plan.steps["up0"], 0,
                  lambda o, k: (XH[:, k if o < 14 else KKV + k, :], XL[:, k if o < 14 else KKV + k, :]),
                  token_major={6 + b: b for b in range(8)} | {10 + b: b for b in range(4)},
                  ready=lambda o, k, i: (signal("c_lo"), (k if o < 14 else KKV + k) + 1, (k, o < 14)),
                  after={14 + h + 1: [rotate_query(h)] for h in range(NH - 1)})
            rotate_query(NH - 1)()
            attention("mla", (drained, plan.out0["wo0"]), (signal("q0_done"), NH))
            dense(lambda _: plan.steps["wo0"], 0, operand(XH, XL), ready=heads_ready("mla"))
            mlp("mlp0")

            dense(lambda _: plan.steps["in1"], 0, operand(XH, XL), token_major={2 + b: b for b in range(NT)},
                  ready=lambda o, k, i: (signal("in1_x_lo"), k + 1, k),
                  after={0: [sums("in1")], 1: [scales("in1")]})
            attention("swa", (drained, plan.out0["wo1"]), (signal("dist_done"), 1))
            dense(lambda _: plan.steps["wo1"], 0, operand(XH, XL), ready=heads_ready("swa"))
            mlp("mlp1")
            sums("final")()
            scales("final")()

            def head_sums(j):
                pe.wait_ge(signal("head_squares"), j + 1)
                if j:
                    pe.wait_ge(signal("head_var"), j)
                pe.matmul(BANK[6][:], const("head_ones", 0, P), ACC[:], start=True, stop=True
                          ).then_inc(signal("head_sums"), 1)

            def head_rotate(j):
                pe.wait_ge(signal("head_normed"), j + 1)
                if j:
                    pe.wait_ge(signal("head_rotated_read"), j)
                pe.matmul(BANK[7][:], const("rot128", 0, P), TMP[:, 0, :], start=True, stop=True
                          ).then_inc(signal("head_rotated"), 1)

            def compress(step):
                if step == 1:
                    pe.wait_ge(signal("w_cmp_in"), 32)
                    for x_ in range(2):
                        for j in range(16):
                            pe.matmul(BANK[4][0:HD, 64 * x_:64 * x_ + 2 * NCMP].rearrange("p (g n) -> p g n", g=NG),
                                      W1[:, x_, j, :], KCS[:, x_, :, 2 * j:2 * j + 16 * (NCMP - 1) + 1:16],
                                      start=j == 0, stop=j == 15)
                    for x_, pe_name in enumerate(("pe_k", "pe_v")):
                        for j in range(16):
                            ins = pe.matmul(BANK[4][0:HD, 128 + x_:129 + x_], W1[:, x_, j, :], gain(pe_name, j),
                                            start=j == 0, stop=j == 15)
                    ins.then_inc(signal("cmp_hidden"), 1)
                elif step == 2:
                    pe.wait_ge(signal("cmp_silu"), 2)
                    pe.matmul(BANK[4][0:HD, 256:256 + 2 * NCMP], W2[:, 0, :], H1[:, 0, 0:2 * NCMP], start=True, stop=True)
                    for g in range(NG):
                        ins = pe.matmul(BANK[4][0:NCMP, 320 + HD * g:320 + HD * (g + 1)],
                                        H1[:, 1, g * NCMP:(g + 1) * NCMP], W2[:, 1, :], start=True, stop=True)
                    ins.then_inc(signal("cmp_out"), 1)
                else:
                    pe.wait_ge(signal("cmp_squares"), 1)
                    pe.matmul(BANK[4][0:HD, 128:128 + 2 * NCMP], ONES[0:HD, 0:HD], KCT[:, 1, 0:2 * NCMP],
                              start=True, stop=True).then_inc(signal("cmp_sums"), 1)

            after, last = {0: [sums("norm1")], 1: [scales("norm1")]}, None
            for what, j in IN2:
                if what == "out":
                    last = j
                else:
                    step = {"norm": head_sums, "rotate": head_rotate, "compress": compress}[what]
                    after.setdefault(last, []).append(lambda step=step, j=j: step(j))
            dense(lambda _: plan.steps["in2"], 0, operand(XH, XL),
                  token_major={8 + b: b for b in range(NT)} | {12 + b: b for b in range(NT)},
                  ready=lambda o, k, i: (signal("in2_x_lo"), k + 1, k), after=after)
            attention("nsa", (drained, plan.out0["merge"]), (signal("kc_done"), 1), (signal("gate_done"), NT),
                      (signal("head_done"), 6), (signal("ya_lo"), 4))

            def merge_operand(o, k):
                hi, lo = [(XH, XL), (XH, XL), (YAH, YAL), (YBH, YBL)][o % 4]
                return hi[:, k, :], lo[:, k, :]

            dense(lambda _: plan.steps["merge"], 0, merge_operand,
                  ready=lambda o, k, i: (signal("nsa_lo"), 2 * k + 2, k) if o % 4 == 3 else None)
            dense(lambda _: plan.steps["wo2"], 0, operand(MIXH, MIXL),
                  ready=lambda o, k, i: (signal("mix_lo"), k + 1, k))

            ffn = plan.steps["ffn_up"]
            per = 4 * KD

            def ffn_part(i):
                return ffn[i * per:(i + 1) * per]

            dense.n = FF2 // 2 + 1
            dense(ffn_part, 0, operand(XH, XL), ready=lambda o, k, i: (signal("norm2_x_lo"), k + 1, k),
                  after={0: [sums("norm2")], 1: [scales("norm2")]})
            with pe.Fori(1, FF2 // 2) as i:
                dense(ffn_part, i, operand(XH, XL))
            dense(lambda _: plan.steps["ffn_down"], 0, operand(H2H, H2L),
                  ready=lambda o, k, i: (signal("h2_lo"), k + 1, k))

        @block.scalar
        def _(act):
            act.dma_start(CT[:], consts).then_inc(consts_in, 16)
            act.dma_start(GV[:], gains).then_inc(consts_in, 16)
            act.dma_start(MEM[:], mem).then_inc(mem_in, 16)
            act.dma_start(POSI[:], pos_cols).then_inc(signal("pos_in"), 16)
            act.dma_start(POSB0[:], pos_rows[0]).then_inc(signal("pos_in"), 16)

            ahead = [0]

            def hi_part(tile_of, i, n_iter=NCH):
                slot = tile_of(i if isinstance(i, int) else 1) % RING
                act.wait_ge(raw_in[slot], over(lambda c: 16 * (tile_of(c) // RING + 1), i, n_iter))
                if not (isinstance(i, int) and tile_of(i) < RING):
                    act.wait_ge(products_done, over(lambda c: plan.tile_mark[tile_of(c) - RING], i, n_iter))
                act.activation(WH[:, slot, :], RAW[:, slot, :], ACT.Copy).then_inc(hi_done, 1)

            def keep_ahead(o, tiles=AHEAD):
                while ahead[0] <= min(plan.out_tile[o] + tiles, plan.tiles - 1):
                    n = ahead[0]
                    hi_part(lambda c: n, 0)
                    ahead[0] += 1

            def keep_ahead_in_loop(o, i, ref, per, n_iter):
                while ahead[0] <= plan.out_tile[o] + AHEAD:
                    n = ahead[0]
                    hi_part(lambda c: n + per * (c - ref), i, n_iter)
                    ahead[0] += 1

            def square(norm, m, src, tokens=S):
                g = SQUARES0[norm] + m
                if g:
                    act.wait_ge(added, g)
                act.activation(SQ[:, 0:tokens], src, ACT.Square).then_inc(squared, 1)

            def std(norm, tokens=S):
                act.wait_ge(signal("var_done"), NORM_NO[norm] + 1)
                act.activation(STD[:, 0:tokens // P], VAR[:, 0:tokens // P], ACT.Sqrt).then_inc(std_done, 1)

            def x_hi(stage, norm_gain, m):
                act.activation(XH[:, m, :], X[:, m, :], ACT.Copy, scale=gain(norm_gain, m)
                               ).then_inc(signal(stage + "_x_hi"), 1)

            def attention(name):
                units, prob, pt = ATTENTION[name]
                n = len(units)
                for i in range(n + VALUE_LAG + 1):
                    if i < n:
                        u = units[i]
                        row = prob[i % len(prob)][:, 0:u.nk + (u.sink is not None)]
                        act.wait_ge(signal(name + "_negmax"), i + 1)
                        act.activation(row, row, ACT.Exp, scale=u.scale,
                                       bias=NM[:, i % 4:i % 4 + 1], accum_out=SUM[:, i % 4:i % 4 + 1]
                                       ).then_inc(signal(name + "_exp"), 1)
                    j = i - TURN_LAG
                    if 0 <= j < n:
                        u = units[j]
                        act.wait_ge(signal(name + "_turned"), j + 1)
                        if j >= len(pt):
                            act.wait_ge(signal(name + "_values"), j - len(pt) + 1)
                        w, cols = min(P, u.nk), u.nb * P
                        act.activation(pt[j % len(pt)][0:w, 0:cols], BANK[TURNED[j % len(TURNED)]][0:w, 0:cols],
                                       ACT.Copy).then_inc(signal(name + "_pt"), 1)
                    j = i - VALUE_LAG - 1
                    if j >= 0 and units[j].head_end:
                        u = units[j]
                        act.wait_ge(signal(name + "_values"), j + 1)
                        act.activation(u.head_end[0], BANK[HEAD_OUT[u.head % 2]][0:HD, :], ACT.Copy
                                       ).then_inc(signal(name + "_hi"), 1)

            def output_projection(stage, norm, x_stage):
                o0 = plan.out0[stage]
                for m in range(KD):
                    keep_ahead(o0 + m)
                    act.wait_ge(drained, o0 + m + 1)
                    square(norm, m, X[:, m, :])
                act.wait_ge(products_done, plan.out_mark[o0 + KD - 1])
                for m in range(KD):
                    x_hi(x_stage, norm, m)

            def mlp(name, norm_after, gain_after, stage_after):
                o0, t0 = plan.out0[name], plan.tile0[name]

                def up(i, keep):
                    for m in range(CH + 1):
                        if m < CH:
                            out_of = lambda c: o0 + 16 * c + m
                            keep(m)
                            act.wait_ge(products_done, over(lambda c: plan.out_mark[out_of(c)], i))
                            act.wait_ge(drained, over(lambda c: out_of(c) - 1, i))
                            act.activation(TMP[:, m % 2, :], BANK[(o0 + m) % RING][:], ACT.Relu
                                           ).then_inc(signal(name + "_relu"), 1)
                            if m == 0 and isinstance(i, int) and i == 0:
                                std(name)
                        if m >= 1:
                            act.wait_ge(drained, over(lambda c: o0 + 16 * c + m, i))
                            act.activation(HH[:, m - 1, :], AB[:, (m - 1) % 2, :], ACT.Copy
                                           ).then_inc(signal(name + "_h_hi"), 1)

                def chunk(i):
                    up(i, lambda m: keep_ahead(o0 + 16 * i + m))
                    for m in range(KD):
                        keep_ahead(o0 + 16 * i + 8 + m)
                        if i == NCH - 1:
                            act.wait_ge(signal(name + "_x_added"), KD * (NCH - 1) + m + 1)
                            square(norm_after, m, X[:, m, :])
                            if stage_after:
                                x_hi(stage_after, gain_after, m)

                chunk(0)
                with act.Fori(1, NCH - 1) as i:
                    def keep(m):
                        keep_ahead_in_loop(o0 + 16 + m, i, 1, 16, NCH)
                    up(i, keep)
                    for m in range(KD):
                        keep(8 + m)
                ahead[0] += 16 * (NCH - 3)
                chunk(NCH - 1)

            in0, memo = plan.out0["in0"], plan.out0["mem"]
            act.wait_ge(consts_in, 32)
            act.wait_ge(x_in, 32)
            for m in range(KD):
                x_hi("in0", "attn0", m)
                square("in0", m, X[:, m, :])
                if m < AHEAD:
                    keep_ahead(in0, m)
            keep_ahead(in0)
            std("in0")
            act.wait_ge(mem_in, 16)
            for m in range(KD):
                square("mem", m, MEM[:, m, :], NMEM)
            keep_ahead(in0 + 1)
            act.wait_ge(signal("angles0"), 2)
            act.activation(COS0[:], COS0[:], ACT.Sin).then_inc(signal("sines0"), 1)
            act.activation(SIN0[:], SIN0[:], ACT.Sin).then_inc(signal("sines0"), 1)
            std("mem", NMEM)
            keep_ahead(in0 + 2)
            for m in range(KD):
                act.wait_ge(signal("mem_scaled"), m + 1)
                act.activation(MH_[:, m, :], TMP[:, m % 2, 0:NMEM], ACT.Copy).then_inc(signal("mem_hi"), 1)
                if m % 2:
                    keep_ahead(in0 + 3 + m // 4)

            def c_squares(norm, first):
                for j in range(NORM_K[norm]):
                    square(norm, j, C32[:, first + j, :])

            def c_hi(first, n):
                for j in range(first, first + n):
                    act.wait_ge(signal("c_scaled"), j + 1)
                    act.activation(XH[:, j, :], TMP[:, j % 2, :], ACT.Copy).then_inc(signal("c_hi"), 1)

            keep_ahead(in0 + 4)
            act.wait_ge(drained, in0 + 2)
            c_squares("c_kv", 0)
            for o in range(5, 8):
                keep_ahead(in0 + o)
            std("c_kv")
            keep_ahead(memo)
            act.wait_ge(products_done, plan.out_mark[in0 + 7])
            c_hi(0, KKV)
            c_squares("c_q", KKV)
            keep_ahead(memo + 1)
            std("c_q")
            keep_ahead(memo + 3)
            c_hi(KKV, KQ)
            for o in range(4, 8):
                keep_ahead(memo + o)
            up0 = plan.out0["up0"]
            act.wait_ge(signal("c_lo"), KKV + KQ)
            for o in range(14):
                keep_ahead(up0 + o)
            for h in range(NH):
                keep_ahead(up0 + 14 + h)
                act.wait_ge(products_done, plan.out_mark[up0 + 14 + h])
                if h >= 2:
                    act.wait_ge(signal("q0_rotated"), h - 1)
                act.activation(TMP[0:QK, h % 2, :], BANK[(up0 + 14 + h) % RING][0:QK, :], ACT.Copy
                               ).then_inc(signal("q0_copied"), 1)
            attention("mla")
            output_projection("wo0", "mlp0", "mlp0")
            mlp("mlp0", "in1", "attn1", "in1")

            act.dma_start(POSB1[:], pos_rows[0]).then_inc(signal("pos1_in"), 16)
            in1 = plan.out0["in1"]
            keep_ahead(in1)
            std("in1")
            for o in range(14):
                keep_ahead(in1 + o)
            attention("swa")
            output_projection("wo1", "mlp1", "mlp1")
            mlp("mlp1", "final", None, None)

            act.dma_start(POSB2[:], pos_rows[1]).then_inc(signal("pos2_in"), 16)
            act.dma_start(W1[:], cmp_w1).then_inc(signal("w_cmp_in"), 16)
            act.dma_start(W2[:], cmp_w2).then_inc(signal("w_cmp_in"), 16)
            std("final")
            for m in range(KD):
                act.wait_ge(signal("x_normed"), m + 1)
                x_hi("in2", "norm1", m)
                square("norm1", m, X[:, m, :])
            in2 = plan.out0["in2"]
            keep_ahead(in2)
            std("norm1")
            keep_ahead(in2 + 1)
            act.wait_ge(signal("angles2"), 2)
            act.activation(COS2[:], COS2[:], ACT.Sin).then_inc(signal("sines2"), 1)
            act.activation(SIN2[:], SIN2[:], ACT.Sin).then_inc(signal("sines2"), 1)

            def head_square(j):
                act.wait_ge(drained, in2 + 2 + j + 1)
                if j:
                    act.wait_ge(signal("head_sums"), j)
                else:
                    act.wait_ge(scale_done, NORM_NO["norm1"] + 1)
                act.activation(ACC[:], R32[:, j, :], ACT.Square).then_inc(signal("head_squares"), 1)

            last = 0
            for what, j in IN2:
                if what == "out":
                    keep_ahead(in2 + j)
                    last = j
                    if j == 2:
                        head_square(0)
                    if j == 15:
                        for b in range(NT):
                            act.wait_ge(drained, in2 + 12 + b + 1)
                            act.activation(GATE[:, b, :], GATE[:, b, :], ACT.Sigmoid).then_inc(signal("gate_sigmoid"), 1)
                    if j >= 18 and (j - 16) % 3 == 2:
                        m = (j - 16) // 3
                        act.wait_ge(signal("ya_done"), m + 1)
                        act.activation(YAH[:, m, :], PT2[:, m % 2, :], ACT.Copy).then_inc(signal("ya_hi"), 1)
                elif what == "norm":
                    act.wait_ge(signal("head_var"), j + 1)
                    act.activation(SQ[:], SQ[:], ACT.Sqrt).then_inc(signal("head_std"), 1)
                    if j < 5:
                        head_square(j + 1)
                elif what == "compress" and j == 1:
                    act.wait_ge(signal("cmp_bias"), 1)
                    for x_ in range(2):
                        act.activation(H1[:, x_, 0:2 * NCMP], BANK[4][0:HD, 64 * x_:64 * x_ + 2 * NCMP], ACT.Silu,
                                       bias=CB[0:HD, x_:x_ + 1]).then_inc(signal("cmp_silu"), 1)
                elif what == "compress" and j == 3:
                    act.wait_ge(signal("cmp_var"), 1)
                    act.activation(KC[:, 0:2 * NCMP], KC[:, 0:2 * NCMP], ACT.Sqrt).then_inc(signal("cmp_std"), 1)
            attention("nsa")

            mo = plan.out0["merge"]
            for m in range(KD):
                for g in range(2):
                    keep_ahead(mo + 4 * m + g)
                    act.wait_ge(drained, mo + 4 * m + g + 1)
                    act.activation(TMP[:, g, :], TMP[:, g, :], ACT.Sigmoid).then_inc(signal("merge_gate"), 1)
                keep_ahead(mo + 4 * m + 3)
                act.wait_ge(signal("mix_done"), m + 1)
                act.activation(MIXH[:, m, :], TMP[:, 0, :], ACT.Copy).then_inc(signal("mix_hi"), 1)
            output_projection("wo2", "norm2", "norm2")

            fo = plan.out0["ffn_up"]

            def ffn_body(i, keep, first=False):
                for j in range(2):
                    keep(2 * j)
                    if first and j == 0:
                        std("norm2")
                    act.wait_ge(signal("conv_done"), over(lambda c: 2 * c + j + 1, i, FF2 // 2 + 1))
                    b = GV[:, GAIN["ffn_b"] + j + 2 * i:GAIN["ffn_b"] + j + 2 * i + 1] if isinstance(i, int) else \
                        GV[:, bass.ds(i * 2 + (GAIN["ffn_b"] + j), 1)]
                    act.activation(TMP[:, 1, :], TMP[:, 0, :], ACT.Silu, bias=b).then_inc(signal("silu_done"), 1)
                    keep(2 * j + 1)
                    act.wait_ge(signal("h2_done"), over(lambda c: 2 * c + j + 1, i, FF2 // 2 + 1))
                    dst = H2H[:, 2 * i + j, :] if isinstance(i, int) else \
                        H2H[:, bass.ds(i * 2 + j, 1), :].rearrange("p a n -> p (a n)")
                    act.activation(dst, SQ[:], ACT.Copy).then_inc(signal("h2_hi"), 1)

            ffn_body(0, lambda q: keep_ahead(fo + q), first=True)
            with act.Fori(1, FF2 // 2) as i:
                ffn_body(i, lambda q: keep_ahead_in_loop(fo + 4 + q, i, 1, 4, FF2 // 2 + 1))
            ahead[0] += 4 * (FF2 // 2 - 2)
            for m in range(KD):
                keep_ahead(plan.out0["ffn_down"] + m)

        @block.vector
        def _(dve):
            own = Order(dve, signal("dve_own"))

            def add_square(norm, m, tokens=S):
                g = SQUARES0[norm] + m
                dve.wait_ge(squared, g + 1)
                if m == 0:
                    ins = dve.tensor_copy(ACC[:, 0:tokens], SQ[:, 0:tokens])
                else:
                    dve.wait_ge(added, g)
                    ins = dve.tensor_tensor(ACC[:, 0:tokens], ACC[:, 0:tokens], SQ[:, 0:tokens], ALU.add)
                ins.then_inc(added, 1)

            def scale_columns(norm, width, tokens=S):
                n, nt = NORM_NO[norm], tokens // P
                dve.wait_ge(sums_done, n + 1)
                dve.tensor_scalar(VAR[:, 0:nt], BANK[4][:, 0:nt], 1.0 / width, EPS, ALU.mult, ALU.add
                                  ).then_inc(signal("var_done"), 1)
                dve.wait_ge(std_done, n + 1)
                own.then(dve.reciprocal(RCOL[:, 0:nt], STD[:, 0:nt]))
                for t in range(nt):
                    ins = dve.tensor_scalar(ACC[:, blk(t)], IDENT, RCOL[:, t:t + 1], None, ALU.mult)
                    if t < nt - 1:
                        own.step(ins)
                ins.then_inc(diag_done, 1)

            def scale_rows(norm, dst, tokens=S):
                n = NORM_NO[norm]
                dve.wait_ge(scale_done, n + 1)
                dve.tensor_copy(dst[:, 0:tokens], BANK[5][:, 0:tokens]).then_inc(scale_used, 1)
                dve.wait_ge(scale_used, n + 1)

            def x_lo(stage, norm_gain, m):
                dve.wait_ge(signal(stage + "_x_hi"), m + 1)
                dve.scalar_tensor_tensor(XL[:, m, :], X[:, m, :], gain(norm_gain, m), XH[:, m, :].bitcast(F32),
                                         ALU.mult, ALU.subtract).then_inc(signal(stage + "_x_lo"), 1)

            def output(o):
                dve.wait_ge(products_done, plan.out_mark[o])
                return BANK[o % RING]

            def both_halves(o, dst, j, by=None):
                bank = output(o)
                for half in range(2):
                    rows = slice(HD * half, HD * half + HD)
                    if by is None:
                        ins = dve.tensor_copy(dst[:, 2 * j + half, :], bank[rows, 0:dst.shape[-1]])
                    else:
                        ins = dve.tensor_tensor(dst[:, 2 * j + half, :], bank[rows, :], by[rows, :], ALU.mult)
                    if not half:
                        own.step(ins)
                ins.then_inc(drained, 1)

            def angles(pos, posf, inv, angle, turns, cos, sin, done):
                c1 = TWO_PI_PARTS
                own.then(dve.tensor_copy(posf, pos))
                own.then(dve.tensor_scalar(angle, posf, inv, None, ALU.mult))
                for dst, quarter in ((cos, 0.25), (sin, 0.0)):
                    own.then(dve.tensor_scalar(turns, angle, 1.0 / (2 * np.pi), quarter, ALU.mult, ALU.add))
                    own.then(dve.tensor_scalar(turns, turns, MAGIC, -MAGIC, ALU.add, ALU.add))
                    own.then(dve.scalar_tensor_tensor(dst, turns, -c1[0], angle, ALU.mult, ALU.add))
                    own.then(dve.scalar_tensor_tensor(dst, turns, -c1[1], dst, ALU.mult, ALU.add))
                    own.then(dve.scalar_tensor_tensor(dst, turns, -c1[2], dst, ALU.mult, ALU.add))
                    own.then(dve.tensor_scalar(dst, dst, 2 * np.pi * quarter, PI_MAX, ALU.add, ALU.min))
                    dve.tensor_scalar(dst, dst, -PI_MAX, None, ALU.max).then_inc(signal(done), 1)

            def attention(name):
                units, prob, pt = ATTENTION[name]
                n = len(units)
                for i in range(n + VALUE_LAG + 2):
                    if i < n:
                        u = units[i]
                        c = i % 4
                        bank, row = BANK[SCORES[i % len(SCORES)]], prob[i % len(prob)]
                        dve.wait_ge(signal(name + "_scores"), i + 1)
                        if i >= len(prob):
                            dve.wait_ge(signal(name + "_turned"), i - len(prob) + 1)
                        if u.bias:
                            dist, slope = u.bias
                            dve.scalar_tensor_tensor(row[:, 0:u.nk], dist, slope, bank[:, 0:u.nk],
                                                     ALU.mult, ALU.add).then_inc(signal(name + "_biased"), 1)
                            own.step(dve.tensor_copy(row[:, u.nk:u.nk + 1], u.sink))
                            dve.wait_ge(signal(name + "_biased"), i + 1)
                            own.wait()
                            own.then(dve.reduce_max(MX[:, c:c + 1], row[:, 0:u.nk + 1], AXX))
                        else:
                            dve.tensor_tensor_reduce(row[:, 0:u.nk], bank[:, 0:u.nk], u.mask, 1.0, -3e38,
                                                     ALU.add, ALU.max, MX[:, c:c + 1]
                                                     ).then_inc(signal(name + "_biased"), 1)
                            dve.wait_ge(signal(name + "_biased"), i + 1)
                        dve.tensor_scalar(NM[:, c:c + 1], MX[:, c:c + 1], -u.scale, None, ALU.mult
                                          ).then_inc(signal(name + "_negmax"), 1)
                    if 1 <= i <= n:
                        u = units[i - 1]
                        c = (i - 1) % 4
                        dve.wait_ge(signal(name + "_exp"), i)
                        own.then(dve.reciprocal(RS[:, c:c + 1], SUM[:, c:c + 1]))
                        row = prob[(i - 1) % len(prob)][:, 0:u.nk]
                        if u.weight is not None:
                            dve.tensor_scalar(row, row, RS[:, c:c + 1], u.weight, ALU.mult, ALU.mult
                                              ).then_inc(signal(name + "_prob"), 1)
                        else:
                            dve.tensor_scalar(row, row, RS[:, c:c + 1], None, ALU.mult
                                              ).then_inc(signal(name + "_prob"), 1)
                    j = i - VALUE_LAG - 2
                    if j >= 0 and units[j].head_end:
                        u = units[j]
                        hi, lo = u.head_end
                        dve.wait_ge(signal(name + "_hi"), u.head + 1)
                        dve.tensor_tensor(lo, BANK[HEAD_OUT[u.head % 2]][0:HD, :], hi.bitcast(F32), ALU.subtract
                                          ).then_inc(signal(name + "_lo"), 1)

            def output_projection(stage, norm, x_stage):
                o0 = plan.out0[stage]
                for m in range(KD + 1):
                    if m < KD:
                        bank = output(o0 + m)
                        dve.tensor_tensor(X[:, m, :], X[:, m, :], bank[:], ALU.add).then_inc(drained, 1)
                    if m >= 1:
                        add_square(norm, m - 1)
                dve.wait_ge(drained, o0 + KD)
                for m in range(KD):
                    x_lo(x_stage, norm, m)

            def mlp(name, norm_after, gain_after, stage_after):
                o0 = plan.out0[name]

                def chunk(i):
                    static = isinstance(i, int)
                    for m in range(CH + 1):
                        if m < CH:
                            dve.wait_ge(signal(name + "_relu"), over(lambda c: CH * c + m + 1, i))
                            if not (static and i == 0 and m < 2):
                                dve.wait_ge(signal(name + "_h_lo"), over(lambda c: CH * c + m - 1, i))
                            dve.tensor_tensor(AB[:, m % 2, :], TMP[:, m % 2, :], TMP[:, m % 2, :], ALU.mult
                                              ).then_inc(drained, 1)
                        if static and i == 0 and m == 0:
                            scale_columns(name, D)
                        if static and i == 0 and m == 2:
                            scale_rows(name, RBC)
                            own.then(dve.tensor_tensor(RB2[:], RBC[:], RBC[:], ALU.mult))
                        if m >= 1:
                            dve.wait_ge(signal(name + "_h_hi"), over(lambda c: CH * c + m, i))
                            dve.tensor_tensor(HL[:, m - 1, :], AB[:, (m - 1) % 2, :], HH[:, m - 1, :].bitcast(F32),
                                              ALU.subtract).then_inc(signal(name + "_h_lo"), 1)
                    for m in range(KD + 1):
                        if m < KD:
                            out_of = lambda c: o0 + 16 * c + 8 + m
                            dve.wait_ge(products_done, over(lambda c: plan.out_mark[out_of(c)], i))
                            if not (static and i == 0 and m < 2):
                                dve.wait_ge(signal(name + "_x_added"), over(lambda c: KD * c + m - 1, i))
                            dve.tensor_tensor(DT[:, m % 2, :], BANK[(o0 + 8 + m) % RING][:], RB2[:], ALU.mult
                                              ).then_inc(drained, 1)
                            dve.wait_ge(drained, over(lambda c: out_of(c) + 1, i))
                            dve.tensor_tensor(X[:, m, :], X[:, m, :], DT[:, m % 2, :], ALU.add
                                              ).then_inc(signal(name + "_x_added"), 1)
                        if static and i == NCH - 1 and m >= 1:
                            add_square(norm_after, m - 1)
                            if stage_after:
                                x_lo(stage_after, gain_after, m - 1)

                chunk(0)
                with dve.Fori(1, NCH - 1) as i:
                    chunk(i)
                chunk(NCH - 1)

            in0, memo = plan.out0["in0"], plan.out0["mem"]
            dve.wait_ge(consts_in, 32)
            dve.wait_ge(x_in, 32)
            for m in range(KD):
                x_lo("in0", "attn0", m)
                add_square("in0", m)
            scale_columns("in0", D)
            dve.wait_ge(signal("pos_in"), 32)
            angles(POSB0[:], POSF0[:], const("inv_mla"), ANG0[:, 0, :], ANG0[:, 1, :], COS0[:], SIN0[:], "angles0")
            scale_rows("in0", RBC)
            for m in range(KD):
                add_square("mem", m, NMEM)

            def c_out(j):
                dve.tensor_tensor(C32[:, j, :], output(in0 + j)[:], RBC[:], ALU.mult).then_inc(drained, 1)

            c_out(0)
            scale_columns("mem", D, NMEM)
            c_out(1)
            scale_rows("mem", ACC, NMEM)
            for m in range(KD + 1):
                if m < KD:
                    if m >= 2:
                        dve.wait_ge(signal("mem_lo"), m - 1)
                    dve.scalar_tensor_tensor(TMP[:, m % 2, 0:NMEM], MEM[:, m, :], gain("mem", m), ACC[:, 0:NMEM],
                                             ALU.mult, ALU.mult).then_inc(signal("mem_scaled"), 1)
                if m >= 1:
                    dve.wait_ge(signal("mem_hi"), m)
                    dve.wait_ge(signal("mem_scaled"), m)
                    dve.tensor_tensor(ML_[:, m - 1, :], TMP[:, (m - 1) % 2, 0:NMEM], MH_[:, m - 1, :].bitcast(F32),
                                      ALU.subtract).then_inc(signal("mem_lo"), 1)
                if m == 4:
                    c_out(2)
            c_out(3)
            c_out(4)
            add_square("c_kv", 0)
            add_square("c_kv", 1)
            dve.tensor_tensor(KR[HD:QK, :], output(in0 + 5)[HD:QK, :], RBC[HD:QK, :], ALU.mult).then_inc(drained, 1)
            both_halves(in0 + 6, QX, 0, RBC)
            both_halves(in0 + 7, QX, 1, RBC)

            def c_scale(norm, first):
                n = NORM_K[norm]
                for j in range(first, first + n + 1):
                    if j < first + n:
                        if j >= 2:
                            dve.wait_ge(signal("c_lo"), j - 1)
                        dve.scalar_tensor_tensor(TMP[:, j % 2, :], C32[:, j, :], gain(norm, j - first), ACC[:],
                                                 ALU.mult, ALU.mult).then_inc(signal("c_scaled"), 1)
                    if j > first:
                        dve.wait_ge(signal("c_hi"), j)
                        dve.wait_ge(signal("c_scaled"), j)
                        dve.tensor_tensor(XL[:, j - 1, :], TMP[:, (j - 1) % 2, :], XH[:, j - 1, :].bitcast(F32),
                                          ALU.subtract).then_inc(signal("c_lo"), 1)

            def mem_out(o):
                l, q = o // 4, o % 4
                if q < 2:
                    both_halves(memo + o, KM[:, l, :, :], q)
                else:
                    dve.tensor_copy(VM[:, l, q - 2, :], output(memo + o)[:, 0:MH * HD]).then_inc(drained, 1)

            scale_columns("c_kv", P * KKV)
            scale_rows("c_kv", ACC)
            c_scale("c_kv", 0)
            mem_out(0)
            for j in range(KQ):
                add_square("c_q", j)
            mem_out(1)
            scale_columns("c_q", P * KQ)
            mem_out(2)
            mem_out(3)
            scale_rows("c_q", ACC)
            c_scale("c_q", KKV)
            for o in range(4, 8):
                mem_out(o)

            dve.wait_ge(signal("sines0"), 2)
            own.step(dve.memset(COS0[0:HD, :], 1.0))
            own.then(dve.memset(SIN0[0:HD, :], 0.0))
            dve.wait_ge(signal("key_rotated"), 1)
            own.then(dve.tensor_tensor(KR[HD:QK, :], KR[HD:QK, :], COS0[HD:QK, :], ALU.mult))
            own.then(dve.tensor_tensor(SQ[HD:QK, :], BANK[6][HD:QK, :], SIN0[HD:QK, :], ALU.mult))
            own.then(dve.tensor_tensor(KR[HD:QK, :], KR[HD:QK, :], SQ[HD:QK, :], ALU.add))
            for h in range(NH):
                ins = dve.tensor_copy(KT0[HD:QK, h, :], KR[HD:QK, :])
                if h < NH - 1:
                    own.step(ins)
            ins.then_inc(signal("key_placed"), 1)
            up0 = plan.out0["up0"]
            for m in range(6):
                both_halves(up0 + m, KT0[0:HD, :, :], m)
            for b in range(NT):
                dve.tensor_copy(V0[:, b, S:NH * HD], output(up0 + 6 + b)[:, 0:NH * HD - S]).then_inc(drained, 1)
            for b in range(NT):
                dve.tensor_copy(V0[:, b, 0:S], output(up0 + 10 + b)[:]).then_inc(drained, 1)
            dve.wait_ge(signal("key_placed"), 1)
            for h in range(NH + 1):
                if h < NH:
                    dve.wait_ge(signal("q0_copied"), h + 1)
                    dve.tensor_tensor(QT0[:, h, :], BANK[(up0 + 14 + h) % RING][0:QK, :], COS0[0:QK, :], ALU.mult
                                      ).then_inc(drained, 1)
                if h >= 1:
                    dve.wait_ge(signal("q0_rotated"), h)
                    if h >= 2:
                        dve.wait_ge(signal("q0_done"), h - 1)
                    dve.tensor_tensor(SQ[0:QK, :], BANK[6 + (h - 1) % 2][0:QK, :], SIN0[0:QK, :], ALU.mult
                                      ).then_inc(signal("q0_rotated_read"), 1)
                    dve.wait_ge(signal("q0_rotated_read"), h)
                    dve.wait_ge(drained, up0 + 14 + h)
                    dve.tensor_tensor(QT0[:, h - 1, :], QT0[:, h - 1, :], SQ[0:QK, :], ALU.add
                                      ).then_inc(signal("q0_done"), 1)
            attention("mla")
            output_projection("wo0", "mlp0", "mlp0")
            mlp("mlp0", "in1", "attn1", "in1")

            in1 = plan.out0["in1"]
            scale_columns("in1", D)
            scale_rows("in1", RBC)
            for m in range(2):
                both_halves(in1 + m, K1, m, RBC)
            for b in range(NT):
                dve.tensor_scalar(V1[:, b, :], output(in1 + 2 + b)[:, 0:NKV * HD], RCOL[:, b:b + 1], None, ALU.mult
                                  ).then_inc(drained, 1)
            dve.wait_ge(signal("pos1_in"), 16)
            own.step(dve.tensor_copy(POSQ, POSI[:, 0, :]))
            own.step(dve.tensor_scalar(SINK8, GV[:, GAIN["sinks"]:GAIN["sinks"] + NH], 1.0 / SCALE, None, ALU.mult))
            own.then(dve.tensor_copy(POSF1[:], POSB1[:]))
            for b in range(NT):
                lo_, k0 = (P, 0) if b == 0 else (0, (b - 1) * P)
                own.step(dve.tensor_scalar(DIST[:, b, lo_:2 * P], POSF1[:, k0:k0 + 2 * P - lo_], -1.0,
                                           POSQ[:, b:b + 1], ALU.mult, ALU.add))
            own.wait()
            for b in range(NT):
                lo_ = P if b == 0 else 0
                ins = dve.tensor_tensor(DIST[:, b, lo_:2 * P], DIST[:, b, lo_:2 * P], const("band", lo_, 2 * P - lo_),
                                        ALU.add)
                if b < NT - 1:
                    own.step(ins)
            ins.then_inc(signal("dist_done"), 1)
            for m in range(6):
                both_halves(in1 + 6 + m, Q1, m, RBC)
            for m in range(2):
                both_halves(in1 + 12 + m, QX, m, RBC)
            dve.wait_ge(signal("dist_done"), 1)
            attention("swa")
            output_projection("wo1", "mlp1", "mlp1")
            mlp("mlp1", "final", None, None)

            scale_columns("final", D)
            scale_rows("final", RBC)
            for m in range(KD):
                dve.scalar_tensor_tensor(X[:, m, :], X[:, m, :], gain("final", m), RBC[:], ALU.mult, ALU.mult
                                         ).then_inc(signal("x_normed"), 1)
                if m >= 1:
                    add_square("norm1", m - 1)
                    x_lo("in2", "norm1", m - 1)
            dve.wait_ge(signal("x_normed"), KD)
            add_square("norm1", KD - 1)
            x_lo("in2", "norm1", KD - 1)
            dve.wait_ge(signal("pos2_in"), 16)
            own.step(dve.memset(UP[:, 0:2], 0.0))
            angles(POSB2[:], POSF2[:], const("inv_nsa"), PROB2[:, 0, :], PROB2[:, 1, :], COS2[:], SIN2[:], "angles2")
            scale_columns("norm1", D)
            scale_rows("norm1", RBC)
            in2 = plan.out0["in2"]

            def in2_out(o):
                if o == 11 or o == 15:
                    for b in range(NT):
                        bank = output(in2 + o - 3 + b)
                        dst = VN[:, b, :] if o == 11 else GATE[:, b, :]
                        dve.tensor_scalar(dst, bank[:, 0:dst.shape[-1]], RCOL[:, b:b + 1], None, ALU.mult
                                          ).then_inc(drained, 1)
                    return
                bank = output(in2 + o)
                if o < 2:
                    for g in range(NG):
                        rows = slice(HD * g, HD * g + HD)
                        own.step(dve.tensor_tensor(KCS[0:HD, o, g, :], bank[rows, :], RBC[rows, :], ALU.mult))
                        ins = dve.tensor_tensor(KCS[HD:P, o, g, 0:S - 1], bank[rows, 1:S], RBC[rows, 1:S], ALU.mult)
                        if g == 0:
                            own.step(ins)
                    ins.then_inc(drained, 1)
                elif o < 8:
                    dve.tensor_tensor(R32[:, o - 2, :], bank[:], RBC[:], ALU.mult).then_inc(drained, 1)
                else:
                    m, q = (o - 16) // 3, (o - 16) % 3
                    if m and q == 0:
                        dve.wait_ge(signal("ya_done"), m)
                    dve.tensor_tensor(PROB2[:, (0, 1, 1)[q], :], bank[:], RBC[:], ALU.mult).then_inc(drained, 1)
                    if q == 1:
                        dve.wait_ge(drained, in2 + o + 1)
                        own.then(dve.tensor_tensor(UP[:, 2:S + 2], PROB2[:, 0, :], PROB2[:, 1, :], ALU.mult))
                        convolve(PROB2[:, 0, :], UP, lambda t: gain("conv_a", 3 * m + t))
                    elif q == 2:
                        dve.wait_ge(drained, in2 + o + 1)
                        if m >= 2:
                            dve.wait_ge(signal("ya_lo"), m - 1)
                        dve.tensor_tensor(PT2[:, m % 2, :], PROB2[:, 0, :], PROB2[:, 1, :], ALU.mult
                                          ).then_inc(signal("ya_done"), 1)
                        dve.wait_ge(signal("ya_hi"), m + 1)
                        dve.tensor_tensor(YAL[:, m, :], PT2[:, m % 2, :], YAH[:, m, :].bitcast(F32), ALU.subtract
                                          ).then_inc(signal("ya_lo"), 1)

            def convolve(dst, src, tap, done=None):
                own.then(dve.tensor_scalar(dst, src[:, 0:S], tap(0), None, ALU.mult))
                own.then(dve.scalar_tensor_tensor(dst, src[:, 1:S + 1], tap(1), dst, ALU.mult, ALU.add))
                ins = dve.scalar_tensor_tensor(dst, src[:, 2:S + 2], tap(2), dst, ALU.mult, ALU.add)
                if done:
                    ins.then_inc(done, 1)
                else:
                    own.then(ins)

            def head_norm(j):
                dve.wait_ge(signal("head_sums"), j + 1)
                if j:
                    dve.wait_ge(signal("head_normed"), j)
                dve.tensor_scalar(SQ[:], BANK[6][:], 1.0 / HD, EPS, ALU.mult, ALU.add).then_inc(signal("head_var"), 1)
                dve.wait_ge(signal("head_std"), j + 1)
                own.then(dve.reciprocal(SQ[:], SQ[:]))
                dve.scalar_tensor_tensor(TMP[:, 0, :], R32[:, j, :], gain(("k_sel", "k_win", "q")[min(j, 2)]), SQ[:],
                                         ALU.mult, ALU.mult).then_inc(signal("head_normed"), 1)

            def head_rotated(j):
                if j == 0:
                    dve.wait_ge(signal("sines2"), 2)
                dve.wait_ge(signal("head_rotated"), j + 1)
                if j:
                    dve.wait_ge(signal("head_done"), j)
                dve.tensor_tensor(TMP[:, 1, :], BANK[7][:], SIN2[:], ALU.mult).then_inc(signal("head_rotated_read"), 1)
                dve.wait_ge(signal("head_normed"), j + 1)
                own.then(dve.tensor_tensor(R32[:, j, :], TMP[:, 0, :], COS2[:], ALU.mult))
                dve.wait_ge(signal("head_rotated_read"), j + 1)
                for half in range(2):
                    rows = slice(HD * half, HD * half + HD)
                    dst = KN[:, j, half, :] if j < 2 else QN[:, 2 * (j - 2) + half, :]
                    ins = dve.tensor_tensor(dst, R32[rows, j, :], TMP[rows, 1, :], ALU.add)
                    if not half:
                        own.step(ins)
                ins.then_inc(signal("head_done"), 1)

            def compress(step):
                w = 2 * NCMP
                if step == 1:
                    dve.wait_ge(signal("cmp_hidden"), 1)
                    dve.tensor_copy(CB[0:HD, :], BANK[4][0:HD, 128:130]).then_inc(signal("cmp_bias"), 1)
                elif step == 2:
                    dve.wait_ge(signal("cmp_out"), 1)
                    own.step(dve.tensor_copy(VC[0:NCMP, :], BANK[4][0:NCMP, 320:448]))
                    own.then(dve.tensor_copy(KCT[:, 0, 0:w], BANK[4][0:HD, 256:256 + w]))
                    dve.tensor_tensor(KCT[:, 1, 0:w], KCT[:, 0, 0:w], KCT[:, 0, 0:w], ALU.mult
                                      ).then_inc(signal("cmp_squares"), 1)
                else:
                    dve.wait_ge(signal("cmp_sums"), 1)
                    dve.tensor_scalar(KC[:, 0:w], BANK[4][0:HD, 128:128 + w], 1.0 / HD, EPS, ALU.mult, ALU.add
                                      ).then_inc(signal("cmp_var"), 1)
                    dve.wait_ge(signal("cmp_std"), 1)
                    own.then(dve.reciprocal(KC[:, 0:w], KC[:, 0:w]))
                    dve.scalar_tensor_tensor(KC[:, 0:w], KCT[:, 0, 0:w], gain("k_cmp")[0:HD, :], KC[:, 0:w],
                                             ALU.mult, ALU.mult).then_inc(signal("kc_done"), 1)

            for what, j in IN2:
                {"out": in2_out, "norm": head_norm, "rotate": head_rotated, "compress": compress}[what](j)
                if what == "out" and j == 16:
                    for b in range(NT):
                        dve.wait_ge(signal("gate_sigmoid"), b + 1)
                        gates = GATE[:, b, 0:24:3]
                        dve.tensor_scalar(gates, gates, const("cmp_valid", b), None, ALU.mult
                                          ).then_inc(signal("gate_done"), 1)
            dve.wait_ge(signal("gate_done"), NT)
            attention("nsa")

            mo = plan.out0["merge"]
            for m in range(KD):
                if m:
                    dve.wait_ge(signal("mix_lo"), m)
                for g in range(2):
                    dve.tensor_tensor(TMP[:, g, :], output(mo + 4 * m + g)[:], RBC[:], ALU.mult).then_inc(drained, 1)
                for g in range(2):
                    bank = output(mo + 4 * m + 2 + g)
                    dve.wait_ge(signal("merge_gate"), 2 * m + g + 1)
                    dve.tensor_tensor(TMP[:, g, :], TMP[:, g, :], bank[:], ALU.mult).then_inc(drained, 1)
                dve.wait_ge(drained, mo + 4 * m + 4)
                dve.tensor_tensor(TMP[:, 0, :], TMP[:, 0, :], TMP[:, 1, :], ALU.add).then_inc(signal("mix_done"), 1)
                dve.wait_ge(signal("mix_hi"), m + 1)
                dve.tensor_tensor(MIXL[:, m, :], TMP[:, 0, :], MIXH[:, m, :].bitcast(F32), ALU.subtract
                                  ).then_inc(signal("mix_lo"), 1)
            output_projection("wo2", "norm2", "norm2")

            fo = plan.out0["ffn_up"]
            own.step(dve.memset(GB[:, :, 0:2], 0.0))

            def ffn_body(i, first=False):
                n_iter = FF2 // 2 + 1
                for j in range(2):
                    def out_of(c, up):
                        return fo + 4 * c + 2 * j + up

                    def tap(t):
                        at = GAIN["ffn_conv"] + 3 * j + t
                        return GV[:, at:at + 1] if isinstance(i, int) else GV[:, bass.ds(i * 6 + at, 1)]

                    if first and j == 0:
                        scale_columns("norm2", D)
                        scale_rows("norm2", RBC)
                    dve.wait_ge(products_done, over(lambda c: plan.out_mark[out_of(c, 0)], i, n_iter))
                    dve.tensor_tensor(GB[:, j, 2:S + 2], BANK[(fo + 2 * j) % RING][:], RBC[:], ALU.mult
                                      ).then_inc(drained, 1)
                    dve.wait_ge(drained, over(lambda c: out_of(c, 0) + 1, i, n_iter))
                    convolve(TMP[:, 0, :], GB[:, j, :], tap, signal("conv_done"))
                    dve.wait_ge(products_done, over(lambda c: plan.out_mark[out_of(c, 1)], i, n_iter))
                    if not (isinstance(i, int) and i == 0 and j == 0):
                        dve.wait_ge(signal("h2_lo"), over(lambda c: 2 * c + j, i, n_iter))
                    dve.tensor_tensor(SQ[:], BANK[(fo + 2 * j + 1) % RING][:], RBC[:], ALU.mult).then_inc(drained, 1)
                    dve.wait_ge(drained, over(lambda c: out_of(c, 1) + 1, i, n_iter))
                    dve.wait_ge(signal("silu_done"), over(lambda c: 2 * c + j + 1, i, n_iter))
                    dve.tensor_tensor(SQ[:], SQ[:], TMP[:, 1, :], ALU.mult).then_inc(signal("h2_done"), 1)
                    dve.wait_ge(signal("h2_hi"), over(lambda c: 2 * c + j + 1, i, n_iter))
                    if isinstance(i, int):
                        hi, lo = H2H[:, 2 * i + j, :], H2L[:, 2 * i + j, :]
                    else:
                        hi, lo = (t[:, bass.ds(i * 2 + j, 1), :].rearrange("p a n -> p (a n)") for t in (H2H, H2L))
                    dve.tensor_tensor(lo, SQ[:], hi.bitcast(F32), ALU.subtract).then_inc(signal("h2_lo"), 1)

            own.wait()
            ffn_body(0, first=True)
            start = own.n
            with dve.Fori(1, FF2 // 2) as i:
                own.more = i * 4 - 4
                ffn_body(i)
            assert own.n - start == 4
            own.more, own.n = 0, start + 4 * (FF2 // 2 - 1)
            for m in range(KD):
                bank = output(plan.out0["ffn_down"] + m)
                dve.tensor_tensor(X[:, m, :], X[:, m, :], bank[:], ALU.add).then_inc(drained, 1)


def units(w, n_k, width=P):
    n = w.shape[1] // width
    return w.reshape(n_k, P, n, width).transpose(2, 0, 1, 3).reshape(n * n_k, P, width)


def tiles(blocks, per_tile):
    n, _, width = blocks.shape
    count = -(-n // per_tile)
    out = np.zeros((count, P, TW), np.float32)
    for b in range(n):
        at = b % per_tile * width
        out[b // per_tile, :, at:at + width] = blocks[b]
    return out


def weight_stream(a):
    mla_in = a["mla_w_in"][0]
    q_rank, kv_rank = KQ * P, KKV * P
    key_rope = np.zeros((D, P), np.float32)
    key_rope[:, HD:QK] = mla_in[:, q_rank + kv_rank:q_rank + kv_rank + ROPE]
    out = [tiles(units(w, KD), UPT) for w in (
        mla_in[:, q_rank:q_rank + kv_rank], mla_in[:, :q_rank], key_rope, mla_in[:, q_rank + kv_rank + ROPE:])]
    for l in range(2):
        w = a["w_mem_kv"][l]
        out += [tiles(units(w[:, :MH * HD], KD), UPT), tiles(units(w[:, MH * HD:], KD, 2 * P), 4)]
    ukv = a["mla_w_ukv"][0].reshape(kv_rank, NH, 2 * HD)
    key, value = (np.ascontiguousarray(ukv[:, :, s]).reshape(kv_rank, NH * HD) for s in (slice(0, HD), slice(HD, 2 * HD)))
    k_units = units(key, KKV)
    second = np.concatenate([tiles(k_units[8:], 4)[0][:, :4 * P], tiles(units(value[:, S:], KKV, 256), 2)[0][:, :4 * P]], axis=1)
    out += [tiles(k_units[:8], UPT), second[None], tiles(units(value[:, :S], KKV, S), 2),
            tiles(units(a["mla_w_uq"][0], KQ, QK), 3 * KQ)]

    def mlp(l):
        for c in range(NCH):
            hidden = slice(c * CH * P, (c + 1) * CH * P)
            yield tiles(units(a["mlp_w_up"][l][:, hidden], KD), UPT)
            yield tiles(units(a["mlp_w_down"][l][hidden], CH), UPT)

    out += [tiles(units(a["w_o"][0], KD), UPT), *mlp(0)]
    w = a["swa_w_in"][0]
    nq, nk = NH * HD, NKV * HD
    out += [tiles(units(w[:, nq:nq + nk], KD), UPT), tiles(units(w[:, nq + nk:nq + 2 * nk], KD, 2 * P), 4),
            tiles(units(w[:, :nq], KD), UPT), tiles(units(w[:, nq + 2 * nk:], KD), UPT)]
    out += [tiles(units(a["w_o"][1], KD), UPT), *mlp(1)]
    w = a["w_in_2"][0]
    a_b, a_c, a_x, q, kc, vc, ksl, vsl, kwn, vwn, g_nsa, g_merge = np.split(
        w, np.cumsum([512, 512, 512, 512] + [P] * 6 + [24]), axis=1)
    out += [tiles(units(v, KD), UPT) for v in (kc, vc, ksl, kwn, q)]
    out += [tiles(units(np.concatenate([vsl, vwn], axis=1), KD, 2 * P), 4), tiles(units(g_nsa, KD, 24), KD)]
    for m in range(4):
        out += [tiles(units(v[:, m * P:(m + 1) * P], KD), UPT) for v in (a_c, a_x, a_b)]
    for m in range(KD):
        c = slice(m * P, (m + 1) * P)
        out += [tiles(units(g_merge[:, :D][:, c], KD), UPT), tiles(units(g_merge[:, D:][:, c], KD), UPT),
                tiles(np.concatenate([units(a["w_a_out_2"][0][:, c], 4), units(a["w_b_out_2"][0][:, c], 4)]), UPT)]
    out += [tiles(units(a["w_o_2"][0], KD), UPT)]
    w = a["w_ffn_in_2"][0]
    for m in range(FF2):
        for half in range(2):
            at = (half * FF2 + m) * P
            out += [tiles(units(w[:, at:at + P], KD), UPT)]
    for m in range(KD):
        out += [tiles(units(a["w_ffn_out_2"][0][:, m * P:(m + 1) * P], FF2), UPT)]
    stream = np.concatenate(out)
    assert stream.shape[0] == PLAN.tiles, (stream.shape, PLAN.tiles)
    return stream


def gain_columns(a):
    def cols(v):
        return v.reshape(-1, P).T

    def heads(v):
        return np.concatenate([v, v])[:, None]

    out = {"attn0": cols(a["attn_norm_g"][0]), "attn1": cols(a["attn_norm_g"][1]),
           "mlp0": cols(a["mlp_norm_g"][0]), "mlp1": cols(a["mlp_norm_g"][1]), "mem": cols(a["mem_norm_g"]),
           "final": cols(a["final_norm_g"]), "c_kv": cols(a["mla_kv_norm_g"][0]), "c_q": cols(a["mla_q_norm_g"][0]),
           "norm1": cols(a["norm1_g_2"][0]), "norm2": cols(a["norm2_g_2"][0]), "q": heads(a["q_norm_g_2"][0]),
           "k_cmp": heads(a["k_norm_g_2"][0, 0]), "k_sel": heads(a["k_norm_g_2"][0, 1]),
           "k_win": heads(a["k_norm_g_2"][0, 2]),
           "conv_a": a["conv_a_w_2"][0].reshape(3, 4, P).transpose(2, 1, 0).reshape(P, 12),
           "ffn_conv": a["ffn_conv_w_2"][0].reshape(3, FF2, P).transpose(2, 1, 0).reshape(P, 3 * FF2),
           "ffn_b": cols(a["ffn_conv_b_2"][0]), "sinks": np.broadcast_to(a["swa_sinks"][0][None], (P, NH)),
           "pe_k": cols(a["cmp_k_pe_2"][0].reshape(-1)), "pe_v": cols(a["cmp_v_pe_2"][0].reshape(-1))}
    return np.ascontiguousarray(np.concatenate([out[name] for name in GAIN], axis=1))


def constants():
    p, c = np.arange(P)[:, None], np.arange(P)[None, :]

    def rotation(first, half, n):
        r = np.zeros((P, P), np.float32)
        for run in range(first, first + n * 2 * half, 2 * half):
            for d in range(half):
                r[run + half + d, run + d] = -1.0
                r[run + d, run + half + d] = 1.0
        return r

    def inverse_frequencies(half, at):
        f = np.float32(10000.0) ** (-(np.arange(half, dtype=np.float32) * np.float32(2.0)) / np.float32(2 * half))
        return np.where(at >= 0, f.astype(np.float32)[at % half], 0).astype(np.float32)[:, None]

    rows = np.arange(P)
    end = np.arange(32) * (CMP // 2) + CMP - 1
    t = np.arange(S).reshape(NT, P).T
    cmp_mask = np.where((end[None, None, :] <= t[:, :, None]) & (np.arange(32) < NCMP)[None, None, :], 0, NEG)
    out = {
        "tri": np.concatenate([np.zeros((P, S - P)), np.where(c <= p, 0, NEG)], axis=1),
        "ident": np.eye(P), "ones": np.ones((P, P)), "rot96": rotation(HD, ROPE // 2, 1),
        "head_ones": p // HD == c // HD, "rot128": rotation(0, HD // 2, 2),
        "band": np.concatenate([np.where(c > p, 0, -NEG), np.where(c <= p, 0, -NEG)], axis=1),
        "cmp_mask": cmp_mask.reshape(P, NT * 32), "cmp_valid": t >= CMP - 1,
        "slopes": np.broadcast_to(-8.0 * 2.0 ** (-8.0 * (np.arange(NH) + 1.0) / NH), (P, NH)),
        "inv_mla": inverse_frequencies(ROPE // 2, np.where((rows >= HD) & (rows < QK), (rows - HD) % (ROPE // 2), -1)),
        "inv_nsa": inverse_frequencies(HD // 2, rows % (HD // 2))}
    return np.ascontiguousarray(np.concatenate([out[name].astype(np.float32) for name in CONST], axis=1))


def kernel(**inputs):
    import concourse.bacc as bacc
    from concourse.bass_utils import run_bass_kernel_spmd

    a = {name: np.asarray(v) for name, v in inputs.items()}

    def feature_major(v):
        return np.ascontiguousarray(v[0].T.reshape(KD, P, -1).transpose(1, 0, 2))

    positions = np.stack([a["positions"][0], a["positions_2"][0]])
    arrays = {
        "stream": weight_stream(a), "gains": gain_columns(a), "consts": constants(),
        "x": feature_major(a["x"]), "mem": feature_major(a["mem"]),
        "pos_rows": np.ascontiguousarray(np.broadcast_to(positions[:, None, :], (2, P, S))),
        "pos_cols": np.ascontiguousarray(positions.reshape(2, NT, P).transpose(2, 0, 1)),
        "cmp_w1": np.ascontiguousarray(np.stack(
            [a[n][0].reshape(16, P, HD).transpose(1, 0, 2) for n in ("cmp_k_w1_2", "cmp_v_w1_2")], axis=1)),
        "cmp_w2": np.ascontiguousarray(np.stack([a[n][0] for n in ("cmp_k_w2_2", "cmp_v_w2_2")], axis=1))}
    nc = bacc.Bacc("TRN2", target_bir_lowering=False, num_devices=1)
    args = [nc.dram_tensor(name, v.shape, mybir.dt.from_np(v.dtype), kind="ExternalInput").ap()
            for name, v in arrays.items()]
    out = nc.dram_tensor("out", (P, KD, S), F32, kind="ExternalOutput").ap()
    program(nc, *args, out)
    r = run_bass_kernel_spmd(nc, [arrays], core_ids=[0])
    got = np.asarray(r.results[0]["out"])
    return np.ascontiguousarray(got.transpose(1, 0, 2).reshape(D, S).T)[None]
```

```python
from contextlib import ExitStack

import numpy as np

import concourse.bass as bass
from concourse import mybir

F32 = mybir.dt.float32
F32R = mybir.dt.float32r
I32 = mybir.dt.int32
ALU = mybir.AluOpType
ACT = mybir.ActivationFunctionType
AXX = mybir.AxisListType.X

P = 128
S = 512
NT = S // P
D = 1024
KD = D // P
NMEM = 256
EPS = 1e-6
MASKED = 1e30
HD = 64
NH = 12
MH = 4
ROPE = 32
QK = HD + ROPE
KQ, KKV = 3, 2
NKV = 4
NH2 = 8
NG = 2
CMP = 32
NCMP = (S - CMP) // (CMP // 2) + 1
CH = 8
NCH = 4
FF2 = 22
FF2P = 24
RING = 4
AHEAD = 3
TURN_LAG, VALUE_LAG = 4, 6
GATES, CHANNELS, LAST_V = 8, 9, 24
UPT = 8
TW = UPT * P
MAGIC = float(1.5 * 2 ** 23)
TWO_PI_1 = 6.28125
TWO_PI_2 = round((2 * np.pi - TWO_PI_1) * 2 ** 20) / 2 ** 20
TWO_PI_PARTS = [TWO_PI_1, TWO_PI_2, 2 * np.pi - TWO_PI_1 - TWO_PI_2]
PI_MAX = 3.1415925
SCALE = HD ** -0.5
MLA_SCALE = QK ** -0.5


def columns(sizes):
    at, out = 0, {}
    for name, n in sizes:
        out[name] = at
        at += n
    return out, at


CONST, NCONST = columns([
    ("cmp_valid", NT), ("slopes", NH), ("inv_mla", 1), ("inv_nsa", 1), ("ident", P), ("ones", P), ("tri", S), ("rot96", P), ("head_rows", 32), ("head_spread", P), ("rot128", P),
    ("band", 2 * P), ("cmp_mask", NT * 32)])
CONST_LATE = CONST["tri"]

GAIN, NGAIN = columns([
    ("attn0", KD), ("attn1", KD), ("mlp0", KD), ("mlp1", KD), ("mem", KD), ("final", KD), ("c_kv", KKV),
    ("c_q", KQ), ("norm1", KD), ("norm2", KD), ("q", 1), ("k_cmp", 1), ("k_sel", 1), ("k_win", 1),
    ("conv_a", 3 * 4), ("ffn_conv", 3 * FF2), ("ffn_b", FF2), ("sinks", NH), ("pe_k", 16), ("pe_v", 16)])


class Plan:

    def __init__(self):
        self.steps, self.tile0, self.out0 = {}, {}, {}
        self.tiles = self.outs = 0

    def stage(self, name, tiles, outs, steps):
        self.tile0[name], self.out0[name] = self.tiles, self.outs
        self.steps[name] = [(self.tiles + t, c, w, k, self.outs + o) for t, c, w, k, o in steps]
        self.tiles += tiles
        self.outs += outs

    def count_marks(self):
        every = [s for steps in self.steps.values() for s in steps]
        last_tile, last_out, first_out = {}, {}, {}
        for i, (t, _, _, _, o) in enumerate(every):
            last_tile[t], last_out[o] = i, i
            first_out.setdefault(o, i)
        marks = sorted(set(last_tile.values()) | set(last_out.values()))
        count = {i: n + 1 for n, i in enumerate(marks)}
        self.tile_mark = {t: count[i] for t, i in last_tile.items()}
        self.out_mark = {o: count[i] for o, i in last_out.items()}
        self.out_tile = {o: every[i][0] for o, i in last_out.items()}
        at = 0
        for name, steps in self.steps.items():
            self.steps[name] = [
                s + (at + j in count, first_out[s[4]] == at + j, last_out[s[4]] == at + j)
                for j, s in enumerate(steps)]
            at += len(steps)


def by_output(n_out, n_k, n_kp=None):
    n_kp = n_kp or n_k
    return [((m * n_kp + k) // UPT, (m * n_kp + k) % UPT * P, P, k, m) for m in range(n_out) for k in range(n_k)]


def by_tokens(n_k, width, n_blocks, per_tile):
    return [(k0 // per_tile, (k - k0) * width, width, k, b)
            for k0 in range(0, n_k, per_tile) for b in range(n_blocks) for k in range(k0, k0 + per_tile)]


def shift(steps, tile, out):
    return [(t + tile, c, w, k, o + out) for t, c, w, k, o in steps]


def make_plan():
    p = Plan()
    p.stage("in0", 8, 8, by_output(8, KD))
    mem = []
    for l in range(2):
        mem += shift(by_output(2, KD), 4 * l, 4 * l) + shift(by_tokens(KD, 2 * P, 2, 4), 4 * l + 2, 4 * l + 2)
    p.stage("mem", 8, 8, mem)
    up = by_output(6, KKV)
    up += [(1, 4 * P + k * 256, 256, k, 6 + b) for b in range(NT) for k in range(KKV)]
    up += [(2, k * S, S, k, 10 + b) for b in range(NT) for k in range(KKV)]
    up += [(3 + h // 3, (h % 3 * KQ + k) * QK, QK, k, 14 + h) for h in range(NH) for k in range(KQ)]
    p.stage("up0", 7, 26, up)
    mlp = []
    for c in range(NCH):
        mlp += shift(by_output(CH, KD), 16 * c, 16 * c) + shift(by_output(KD, CH), 16 * c + 8, 16 * c + 8)
    p.stage("wo0", 8, 8, by_output(8, KD))
    p.stage("mlp0", 64, 64, mlp)
    p.stage("in1", 12, 14, by_output(2, KD) + shift(by_tokens(KD, 2 * P, NT, 4), 2, 2) + shift(by_output(8, KD), 4, 6))
    p.stage("wo1", 8, 8, by_output(8, KD))
    p.stage("mlp1", 64, 64, mlp)
    p.stage("in2", 23, 25, by_output(8, KD) + [(8, k * 24, 24, k, GATES) for k in range(KD)]
            + shift(by_output(12, KD), 9, CHANNELS) + shift(by_tokens(KD, 2 * P, NT, 4), 21, 21))
    p.stage("merge", 24, 32, [
        s for m in range(KD) for s in
        shift(by_output(2, KD), 3 * m, 4 * m) + shift(by_output(2, 4), 3 * m + 2, 4 * m + 2)])
    p.stage("wo2", 8, 8, by_output(8, KD))
    p.stage("ffn_up", 2 * FF2, 2 * FF2, by_output(2 * FF2, KD))
    p.stage("ffn_down", FF2P, KD, by_output(KD, FF2, FF2P))
    p.count_marks()
    return p


PLAN = make_plan()
NORMS = [("in0", KD), ("mem", KD), ("c_kv", KKV), ("c_q", KQ), ("mlp0", KD), ("in1", KD), ("mlp1", KD),
         ("final", KD), ("norm1", KD), ("norm2", KD)]
NORM_NO = {name: i for i, (name, _) in enumerate(NORMS)}
SQUARES0 = {name: sum(k for _, k in NORMS[:i]) for i, (name, _) in enumerate(NORMS)}
NORM_K = dict(NORMS)


def over(fn, i, n=NCH):
    if isinstance(i, int):
        return fn(i)
    step = fn(1) - fn(0)
    assert all(fn(j) == fn(0) + j * step for j in range(n - 1))
    return i * step + fn(0) if step else fn(0)


class Order:

    def __init__(self, eng, sem):
        self.eng, self.sem, self.n, self.more = eng, sem, 0, 0

    def step(self, ins):
        ins.then_inc(self.sem, 1)
        self.n += 1

    def wait(self):
        self.eng.wait_ge(self.sem, self.more + self.n)

    def then(self, ins):
        self.step(ins)
        self.wait()


class Unit:

    def __init__(self, q, k, nk, mask, values, out_cols, start=True, stop=True, head_end=None,
                 first=0, sink=False, weight=None):
        self.q, self.k, self.nk, self.mask = q, k, nk, mask
        self.values = values
        self.out_cols = out_cols
        self.start, self.stop = start, stop
        self.head_end = head_end
        self.weight = weight
        self.nb = -(-nk // P)
        self.keys = slice(first, first + nk)
        self.terms = slice(first, first + nk + sink)


def program(nc, stream, gains, consts, x, mem, pos_rows, pos_cols, cmp_w1, cmp_w2, out):
    plan = PLAN
    ctx = ExitStack()
    with ctx:
        def tensor(stack, name, shape, dt=F32):
            return stack.enter_context(nc.sbuf_tensor(name, shape, dt))

        X = tensor(ctx, "X", [P, KD, S])
        XH = tensor(ctx, "XH", [P, KD, S], F32R)
        XL = tensor(ctx, "XL", [P, KD, S], F32R)
        RAW = tensor(ctx, "RAW", [P, RING, TW])
        WH = tensor(ctx, "WH", [P, RING, TW], F32R)
        WL = tensor(ctx, "WL", [P, RING, TW], F32R)
        CT = tensor(ctx, "CT", [P, NCONST])
        GV = tensor(ctx, "GV", [P, NGAIN])
        GF = tensor(ctx, "GF", [P, KD])
        ACC = tensor(ctx, "ACC", [P, S])
        SQ = tensor(ctx, "SQ", [P, S])
        TMP = tensor(ctx, "TMP", [P, 2, S])
        RBC = tensor(ctx, "RBC", [P, S])
        SM = tensor(ctx, "SM", [P, 54])
        POSI = tensor(ctx, "POSI", [P, 2, NT], I32)
        VAR, STD, RCOL, POSQ = SM[:, 0:4], SM[:, 4:8], SM[:, 8:12], SM[:, 12:16]
        LEAST, SUM, RS = SM[:, 16:24], SM[:, 24:32], SM[:, 32:40]
        SINK, CB = SM[:, 40:52], SM[:, 52:54]
        BANK = [ctx.enter_context(nc.psum_tensor(f"bank{i}", [P, S], F32)) for i in range(8)]

        with ExitStack() as block1:
            KM = tensor(block1, "KM", [HD, 2, MH, NMEM])
            VM = tensor(block1, "VM", [P, 2, 2, MH * HD])
            PROB1 = tensor(block1, "PROB1", [P, 3, S])
            PT1 = tensor(block1, "PT1", [P, 2, S])
            QX = tensor(block1, "QX", [HD, MH, S])
            with ExitStack() as mla:
                V0 = tensor(mla, "V0", [P, NT, NH * HD])
                COS0 = tensor(mla, "COS0", [P, S])
                SIN0 = tensor(mla, "SIN0", [P, S])
                with ExitStack() as late:
                    QT0 = tensor(late, "QT0", [QK, NH, S])
                    KT0 = tensor(late, "KT0", [QK, NH, S])
                with ExitStack() as early:
                    C32 = tensor(early, "C32", [P, KKV + KQ, S])
                    KR = tensor(early, "KR", [P, S])
                    POSB0 = tensor(early, "POSB0", [P, S], I32)
                    POSF0 = tensor(early, "POSF0", [P, S])
                    ANG0 = tensor(early, "ANG0", [P, 2, S])
                    MEM = tensor(early, "MEM", [P, KD, NMEM])
                    MH_ = tensor(early, "MH_", [P, KD, NMEM], F32R)
                    ML_ = tensor(early, "ML_", [P, KD, NMEM], F32R)
            with ExitStack() as mlp:
                HH = tensor(mlp, "HH", [P, CH, S], F32R)
                HL = tensor(mlp, "HL", [P, CH, S], F32R)
                RB2 = tensor(mlp, "RB2", [P, S])
                AB = tensor(mlp, "AB", [P, 2, S])
                DT = tensor(mlp, "DT", [P, 2, S])
            with ExitStack() as swa:
                Q1 = tensor(swa, "Q1", [HD, NH, S])
                K1 = tensor(swa, "K1", [HD, NKV, S])
                V1 = tensor(swa, "V1", [P, NT, NKV * HD])
                DIST = tensor(swa, "DIST", [P, NT, 2 * P])
                BIAS = tensor(swa, "BIAS", [P, 2, NT, 2 * P + 1])
                POSB1 = tensor(swa, "POSB1", [P, S], I32)
                POSF1 = tensor(swa, "POSF1", [P, S])
        with ExitStack() as block2:
            YAH = tensor(block2, "YAH", [P, 4, S], F32R)
            YAL = tensor(block2, "YAL", [P, 4, S], F32R)
            with ExitStack() as before:
                R32 = tensor(before, "R32", [P, 6, S])
                KCS = tensor(before, "KCS", [P, 2, NG, S])
                W1 = tensor(before, "W1", [P, 2, 16, HD])
                W2 = tensor(before, "W2", [HD, 2, HD])
                H1 = tensor(before, "H1", [HD, 2, 64])
                PEW = tensor(before, "PEW", [P, 2, HD])
                COS2 = tensor(before, "COS2", [P, S])
                SIN2 = tensor(before, "SIN2", [P, S])
                UP = tensor(before, "UP", [P, S + 2])
                HR = tensor(before, "HR", [P, 2, S])
                POSF2, POSB2 = HR[:, 0, :], HR[:, 1, :].bitcast(I32)
                with ExitStack() as q_k_v:
                    QN = tensor(q_k_v, "QN", [HD, NH2, S])
                    KN = tensor(q_k_v, "KN", [HD, 2, NG, S])
                    VN = tensor(q_k_v, "VN", [P, NT, 2 * P])
                    KC = tensor(q_k_v, "KC", [HD, 64])
                    KCT = tensor(q_k_v, "KCT", [HD, 2, 64])
                    VC = tensor(q_k_v, "VC", [32, P])
                    GATE = tensor(q_k_v, "GATE", [P, NT, 24])
                    PROB2 = tensor(q_k_v, "PROB2", [P, 2, S])
                    PT2 = tensor(q_k_v, "PT2", [P, 2, S])
                    GATE_ROWS = PT2[0:24, 1, :]
                with ExitStack() as merged:
                    MIXH = tensor(merged, "MIXH", [P, KD, S], F32R)
                    MIXL = tensor(merged, "MIXL", [P, KD, S], F32R)
            with ExitStack() as after:
                YBH = tensor(after, "YBH", [P, 4, S], F32R)
                YBL = tensor(after, "YBL", [P, 4, S], F32R)
        with ExitStack() as ffn:
            GB = tensor(ffn, "GB", [P, 2, S + 2])
            H2H = tensor(ffn, "H2H", [P, FF2, S], F32R)
            H2L = tensor(ffn, "H2L", [P, FF2, S], F32R)

        signals = {}

        def signal(name):
            if name not in signals:
                signals[name] = ctx.enter_context(nc.semaphore(name))
            return signals[name]

        raw_in = [signal(f"raw_in{j}") for j in range(RING)]
        hi_done, lo_done = signal("hi_done"), signal("lo_done")
        products_done = signal("products_done")
        drained = signal("drained")
        consts_in, mem_in = signal("consts_in"), signal("mem_in")
        x_in = [signal(f"x_in{j}") for j in range(RING)]
        squared, added = signal("squared"), signal("added")
        sums_done, std_done = signal("sums_done"), signal("std_done")
        diag_done, scale_done = signal("diag_done"), signal("scale_done")
        scale_used = signal("scale_used")

        def const(name, a=0, n=1):
            return CT[:, CONST[name] + a:CONST[name] + a + n]

        def gain(name, j=0):
            if name == "final_norm1":
                return GF[:, j:j + 1]
            return GV[:, GAIN[name] + j:GAIN[name] + j + 1]

        IDENT, ONES, TRI = const("ident", 0, P), const("ones", 0, P), const("tri", 0, S)

        def blk(t, n=1):
            return slice(t * P, (t + n) * P)

        def cross_units(layer):
            return [Unit(QX[:, h, blk(b)], KM[:, layer, h, :], NMEM, TRI[:, 0:NMEM],
                         [VM[:, layer, kb, h * HD:(h + 1) * HD] for kb in range(2)], blk(b),
                         head_end=mix_tile(NH + h) if b == NT - 1 else None)
                    for h in range(MH) for b in range(NT)]

        def mix_tile(h, hi=None, lo=None):
            hi, lo = (XH, XL) if hi is None else (hi, lo)
            rows = slice(HD * (h % 2), HD * (h % 2) + HD)
            return hi[rows, h // 2, :], lo[rows, h // 2, :]

        def mla_units():
            return [Unit(QT0[:, h, blk(b)], KT0[:, h, 0:(b + 1) * P], (b + 1) * P, TRI[:, S - (b + 1) * P:S],
                         [V0[:, kb, h * HD:(h + 1) * HD] for kb in range(b + 1)], blk(b),
                         head_end=mix_tile(h) if b == NT - 1 else None)
                    for h in range(NH) for b in range(NT)] + cross_units(0)

        def swa_units():
            units = []
            for h in range(NH):
                g = h // (NH // NKV)
                for b in range(NT):
                    kb0 = max(b - 1, 0)
                    nk = (b + 1 - kb0) * P
                    first = 2 * P - nk
                    units.append(Unit(
                        Q1[:, h, blk(b)], K1[:, g, kb0 * P:kb0 * P + nk], nk, BIAS[:, h % 2, b, first:],
                        [V1[:, kb, g * HD:(g + 1) * HD] for kb in range(kb0, b + 1)], blk(b),
                        head_end=mix_tile(h) if b == NT - 1 else None, first=first, sink=True))
            return units + cross_units(1)

        def nsa_units():
            units = []
            for h in range(NH2):
                g = h // (NH2 // NG)
                for b in range(NT):
                    def weight(branch):
                        return GATE[:, b, 3 * h + branch:3 * h + branch + 1]
                    units.append(Unit(QN[:, h, blk(b)], KC[:, g * NCMP:(g + 1) * NCMP], NCMP,
                                      const("cmp_mask", b * 32, NCMP),
                                      [VC[0:NCMP, g * HD:(g + 1) * HD]], blk(b), stop=False, weight=weight(0)))
                    for br in range(2):
                        units.append(Unit(
                            QN[:, h, blk(b)], KN[:, br, g, 0:(b + 1) * P], (b + 1) * P, TRI[:, S - (b + 1) * P:S],
                            [VN[:, kb, br * P + g * HD:br * P + (g + 1) * HD] for kb in range(b + 1)], blk(b),
                            start=False, stop=br == 1, weight=weight(1 + br),
                            head_end=mix_tile(h, YBH, YBL) if b == NT - 1 and br == 1 else None))
            return units

        def ring(*tensors):
            return [t[:, j, :] if len(t.shape) == 3 else t[:] for t in tensors
                    for j in range(t.shape[1] if len(t.shape) == 3 else 1)]

        ATTENTION = {"mla": (mla_units(), ring(PROB1, ACC, SQ), ring(PT1, TMP[:, 0:1, :])),
                     "swa": (swa_units(), ring(PROB1, ACC, SQ), ring(PT1, TMP[:, 0:1, :])),
                     "nsa": (nsa_units(), ring(PROB2, ACC, SQ, TMP[:, 1:2, :]), ring(PT2, TMP[:, 0:1, :]))}
        SCORES, TURNED, HEAD_OUT = (0, 1, 2), (3, 4, 7), (5, 6)
        for units, _, _ in ATTENTION.values():
            h = 0
            for u in units:
                u.head = h
                h += u.head_end is not None

        AFTER_OUT = {4: [("sum", 0)], 5: [("sum", 1)], 6: [("sum", 2)], 7: [("sum", 3), ("scale", 0)],
                     8: [("sum", 4), ("spread", 0), ("compress", 1)], 9: [("sum", 5), ("rotate", 0), ("spread", 1)],
                     10: [("rotate", 1), ("compress", 2)], 11: [("spread", 2), ("scale", 1)],
                     12: [("rotate", 2), ("spread", 3), ("compress", 3)], 13: [("rotate", 3), ("spread", 4), ("gates", 0)],
                     14: [("rotate", 4), ("spread", 5)], 15: [("rotate", 5)]}
        IN2 = []
        for o in list(range(CHANNELS + 12)) + [LAST_V]:
            IN2.append(("out", o))
            IN2 += AFTER_OUT.get(o, [])

        block = ctx.enter_context(nc.Block())

        @block.sync
        def _(sp):
            def load(n, slot, source):
                if not (isinstance(n, int) and n < RING):
                    sp.wait_ge(lo_done, n - RING + 1)
                sp.dma_start(RAW[:, slot, :], source).then_inc(raw_in[slot], 16)

            for j in range(RING):
                sp.dma_start(X[:, 2 * j:2 * j + 2, :], x[:, 2 * j:2 * j + 2, :]).then_inc(x_in[j], 16)
                if j == 0:
                    load(0, 0, stream[0])
            for j in range(1, RING):
                load(j, j, stream[j])
            with sp.Fori(1, plan.tiles // RING) as i:
                for j in range(RING):
                    load(i * RING + j, j, stream[bass.ds(i * RING + j, 1)].rearrange("a p n -> p (a n)"))
            for n in range(plan.tiles // RING * RING, plan.tiles):
                load(n, n % RING, stream[n])
            for m in range(KD):
                sp.wait_ge(drained, plan.out0["ffn_down"] + m + 1)
                sp.dma_start(out[:, m, :], X[:, m, :]).then_inc(signal("out_written"), 16)
            sp.wait_ge(signal("out_written"), 16 * KD)

        @block.gpsimd
        def _(pool):
            def lo_part(n, slot):
                pool.wait_ge(hi_done, n + 1)
                pool.tensor_tensor(WL[:, slot, :], RAW[:, slot, :], WH[:, slot, :].bitcast(F32),
                                   ALU.subtract).then_inc(lo_done, 1)

            def lo_parts(start, end):
                a, b = -(-start // RING), end // RING
                for n in range(start, a * RING):
                    lo_part(n, n % RING)
                with pool.Fori(a, b) as i:
                    for j in range(RING):
                        lo_part(i * RING + j, j)
                for n in range(b * RING, end):
                    lo_part(n, n % RING)

            before_swa = plan.out_tile[plan.out0["wo1"] - 1] + AHEAD + 1
            lo_parts(0, before_swa)
            pool.wait_ge(signal("dist_done"), 1)
            for h in range(NH):
                if h >= 2:
                    pool.wait_ge(signal("swa_biased"), NT * (h - 1))
                pool.tensor_scalar(BIAS[:, h % 2, :, 0:2 * P], DIST[:], const("slopes", h), None, ALU.mult
                                   ).then_inc(signal("bias_written"), 1)
                pool.tensor_scalar(BIAS[:, h % 2, :, 2 * P], ONES[:, 0:NT], SINK[:, h:h + 1], None, ALU.mult
                                   ).then_inc(signal("bias_written"), 1)
            lo_parts(before_swa, plan.tiles)

        @block.tensor
        def _(pe):
            def product(dst, lhs, rhs, start, stop):
                pe.matmul(dst, lhs[0], rhs[0], start=start, stop=False)
                pe.matmul(dst, lhs[0], rhs[1], start=False, stop=False)
                return pe.matmul(dst, lhs[1], rhs[0], start=False, stop=stop)

            def dense(steps_of, i, act, n_tok=S, token_major=(), ready=None, after=None, seen=None):
                seen = set() if seen is None else seen
                tiles_seen = set()
                first = steps_of(0 if not isinstance(i, int) else i)
                o0 = first[0][4]
                for j, (t, c, w, k, o, mark, start, stop) in enumerate(first):
                    if start and o >= RING:
                        pe.wait_ge(drained, over(lambda n: steps_of(n)[j][4] - RING + 1, i, dense.n))
                    if ready and (r := ready(o - o0, k, i)) is not None and r[2] not in seen:
                        seen.add(r[2])
                        pe.wait_ge(r[0], r[1])
                    if t not in tiles_seen:
                        tiles_seen.add(t)
                        pe.wait_ge(lo_done, over(lambda n: steps_of(n)[j][0] + 1, i, dense.n))
                    weights = WH[:, t % RING, c:c + w], WL[:, t % RING, c:c + w]
                    bank = BANK[o % RING]
                    if o - o0 in token_major:
                        tok = token_major[o - o0]
                        ins = product(bank[:, 0:w], [a[:, blk(tok)] for a in act(o - o0, k)], weights, start, stop)
                    else:
                        ins = product(bank[0:w, 0:n_tok], weights, act(o - o0, k), start, stop)
                    if mark:
                        ins.then_inc(products_done, 1)
                    if stop and after and o - o0 in after:
                        for step in after[o - o0]:
                            step()

            dense.n = NCH

            def operand(hi, lo, first=0):
                return lambda o, k: (hi[:, first + k, :], lo[:, first + k, :])

            def sums(norm, tokens=S):
                def step():
                    pe.wait_ge(added, SQUARES0[norm] + NORM_K[norm])
                    for t in range(tokens // P):
                        ins = pe.matmul(BANK[4][:, t:t + 1], ACC[:, blk(t)], ONES[:, 0:1], start=True, stop=True)
                    ins.then_inc(sums_done, 1)
                return step

            def scales(norm, tokens=S, diagonal=ACC):
                def step():
                    n = NORM_NO[norm]
                    if n:
                        pe.wait_ge(scale_used, n)
                    pe.wait_ge(diag_done, n + 1)
                    pe.matmul(BANK[5][:, 0:tokens], ONES, diagonal[:, 0:tokens], start=True, stop=True
                              ).then_inc(scale_done, 1)
                return step

            def attention(name, *ready):
                units, prob, pt = ATTENTION[name]
                for sem, value in ready:
                    pe.wait_ge(sem, value)
                rotated = name == "mla"
                n, ns, nt = len(units), len(SCORES), len(TURNED)
                for i in range(n + VALUE_LAG):
                    if i < n:
                        u = units[i]
                        if i >= ns:
                            pe.wait_ge(signal(name + "_biased"), i - ns + 1)
                        if rotated and i < NH * NT and i % NT == 0:
                            pe.wait_ge(signal("q0_done"), u.head + 1)
                        pe.matmul(BANK[SCORES[i % ns]][:, u.keys], u.q, u.k, start=True, stop=True
                                  ).then_inc(signal(name + "_scores"), 1)
                    j = i - TURN_LAG
                    if 0 <= j < n:
                        u = units[j]
                        pe.wait_ge(signal(name + "_prob"), j + 1)
                        if j >= nt:
                            pe.wait_ge(signal(name + "_pt"), j - nt + 1)
                        if rotated and j == 0:
                            pe.wait_ge(signal("q0_rotated_read"), NH)
                        row = prob[j % len(prob)][:, u.keys]
                        for kb in range(u.nb):
                            w = min(P, u.nk - kb * P)
                            ins = pe.transpose(BANK[TURNED[j % nt]][0:w, blk(kb)], row[:, kb * P:kb * P + w], IDENT)
                        ins.then_inc(signal(name + "_turned"), 1)
                    j = i - VALUE_LAG
                    if 0 <= j:
                        u = units[j]
                        pe.wait_ge(signal(name + "_pt"), j + 1)
                        if u.head >= 2 and u.start and (j == 0 or units[j - 1].head != u.head):
                            pe.wait_ge(signal(name + "_lo"), u.head - 1)
                        for kb in range(u.nb):
                            w = min(P, u.nk - kb * P)
                            ins = pe.matmul(BANK[HEAD_OUT[u.head % 2]][0:HD, u.out_cols], u.values[kb],
                                            pt[j % len(pt)][0:w, blk(kb)],
                                            start=u.start and kb == 0, stop=u.stop and kb == u.nb - 1)
                        ins.then_inc(signal(name + "_values"), 1)

            def heads_ready(name):
                return lambda o, k, i: (signal(name + "_lo"), 2 * k + 2, k)

            def mlp(name):
                all_steps = plan.steps[name]
                per = len(all_steps) // NCH // 2

                def part(which):
                    return lambda c: all_steps[(2 * c + which) * per:(2 * c + which + 1) * per]

                def chunk(i, seen, after=None):
                    dense(part(0), i, operand(XH, XL), after=after, seen=seen,
                          ready=lambda o, k, _: (signal(name + "_x_lo"), k + 1, k))
                    dense(part(1), i, operand(HH, HL),
                          ready=lambda o, k, _: (signal(name + "_h_lo"),
                                                 over(lambda c: CH * c + k + 1, i), k))

                chunk(0, set(), {0: [sums(name)], 1: [scales(name)]})
                with pe.Fori(1, NCH - 1) as i:
                    chunk(i, set(range(KD)))
                chunk(NCH - 1, set(range(KD)))

            pe.wait_ge(consts_in, 32)
            dense(lambda _: plan.steps["in0"], 0, operand(XH, XL),
                  ready=lambda o, k, i: (signal("in0_x_lo"), k + 1, k),
                  after={1: [sums("in0")], 2: [scales("in0", diagonal=TMP[:, 0, :])], 3: [sums("mem", NMEM)], 4: [scales("mem", NMEM)],
                         7: [sums("c_kv")]})

            def rotate_key():
                pe.wait_ge(signal("late_consts_in"), 16)
                pe.wait_ge(drained, plan.out0["in0"] + 6)
                pe.matmul(BANK[6][HD:QK, :], const("rot96", HD, ROPE)[HD:QK, :], KR[HD:QK, :], start=True, stop=True
                          ).then_inc(signal("key_rotated"), 1)

            dense(lambda _: plan.steps["mem"], 0, operand(MH_, ML_), n_tok=NMEM,
                  token_major={2: 0, 3: 1, 6: 0, 7: 1},
                  ready=lambda o, k, i: (signal("mem_lo"), k + 1, k),
                  after={0: [scales("c_kv")], 2: [sums("c_q")], 4: [scales("c_q")], 6: [rotate_key]})

            def rotate_query(h):
                def step():
                    pe.wait_ge(signal("q0_copied"), h + 1)
                    if h >= 2:
                        pe.wait_ge(signal("q0_rotated_read"), h - 1)
                    else:
                        pe.wait_ge(signal("key_placed"), NH)
                    pe.matmul(BANK[6 + h % 2][0:QK, :], const("rot96", 0, QK)[0:QK, :], TMP[0:QK, h % 2, :],
                              start=True, stop=True).then_inc(signal("q0_rotated"), 1)
                return step

            dense(lambda _: plan.steps["up0"], 0,
                  lambda o, k: (XH[:, k if o < 14 else KKV + k, :], XL[:, k if o < 14 else KKV + k, :]),
                  token_major={6 + b: b for b in range(8)} | {10 + b: b for b in range(4)},
                  ready=lambda o, k, i: (signal("c_lo"), (k if o < 14 else KKV + k) + 1, (k, o < 14)),
                  after={14 + h + 1: [rotate_query(h)] for h in range(NH - 1)})
            rotate_query(NH - 1)()
            attention("mla", (drained, plan.out0["wo0"]))
            dense(lambda _: plan.steps["wo0"], 0, operand(XH, XL), ready=heads_ready("mla"))
            mlp("mlp0")

            dense(lambda _: plan.steps["in1"], 0, operand(XH, XL), token_major={2 + b: b for b in range(NT)},
                  ready=lambda o, k, i: (signal("in1_x_lo"), k + 1, k),
                  after={0: [sums("in1")], 1: [scales("in1")]})
            attention("swa", (drained, plan.out0["wo1"]), (signal("column_zeroed"), len(SCORES)))
            dense(lambda _: plan.steps["wo1"], 0, operand(XH, XL), ready=heads_ready("swa"))
            mlp("mlp1")

            def head_sum(j):
                pe.wait_ge(signal("head_squares"), j + 1)
                first = 32 * (j % 3)
                pe.matmul(BANK[6 - j // 3][first:first + 32, :], const("head_rows", 0, 32), ACC[:], start=True,
                          stop=True).then_inc(signal("head_sums"), 1)

            def head_spread(j):
                pe.wait_ge(signal("head_scales"), j // 3 + 1)
                if j:
                    pe.wait_ge(signal("head_normed"), j)
                rows = slice(32 * (j % 3), 32 * (j % 3) + 32)
                pe.matmul(BANK[6][:], const("head_spread", 0, P)[rows, :], HR[rows, j // 3, :], start=True, stop=True
                          ).then_inc(signal("head_spread"), 1)

            def head_rotate(j):
                pe.wait_ge(signal("head_normed"), j + 1)
                if j:
                    pe.wait_ge(signal("head_rotated_read"), j)
                pe.matmul(BANK[7][:], const("rot128", 0, P), TMP[:, j % 2, :], start=True, stop=True
                          ).then_inc(signal("head_rotated"), 1)

            def compress(step):
                if step == 1:
                    pe.wait_ge(signal("w_cmp_in"), 32)
                    for x_ in range(2):
                        for j in range(16):
                            pe.matmul(BANK[4][0:HD, 64 * x_:64 * x_ + 2 * NCMP].rearrange("p (g n) -> p g n", g=NG),
                                      W1[:, x_, j, :], KCS[:, x_, :, 2 * j:2 * j + 16 * (NCMP - 1) + 1:16],
                                      start=j == 0, stop=j == 15)
                    pe.wait_ge(signal("positions_weighted"), 2)
                    for x_ in range(2):
                        ins = pe.matmul(BANK[4][0:HD, 128 + x_:129 + x_], PEW[:, x_, :], ONES[:, 0:1],
                                        start=True, stop=True)
                    ins.then_inc(signal("cmp_hidden"), 1)
                elif step == 2:
                    pe.wait_ge(signal("cmp_silu"), 2)
                    pe.matmul(BANK[4][0:HD, 256:256 + 2 * NCMP], W2[:, 0, :], H1[:, 0, 0:2 * NCMP], start=True, stop=True)
                    for g in range(NG):
                        ins = pe.matmul(BANK[4][0:NCMP, 320 + HD * g:320 + HD * (g + 1)],
                                        H1[:, 1, g * NCMP:(g + 1) * NCMP], W2[:, 1, :], start=True, stop=True)
                    ins.then_inc(signal("cmp_out"), 1)
                else:
                    pe.wait_ge(signal("cmp_squares"), 1)
                    pe.matmul(BANK[4][0:HD, 128:128 + 2 * NCMP], ONES[0:HD, 0:HD], KCT[:, 1, 0:2 * NCMP],
                              start=True, stop=True).then_inc(signal("cmp_sums"), 1)

            after = {0: [sums("final")], 1: [scales("final", diagonal=TMP[:, 0, :])],
                     2: [sums("norm1")], 3: [scales("norm1")]}
            def turn_gates(_):
                pe.wait_ge(signal("gate_sigmoid"), 1)
                pe.wait_ge(signal("kc_done"), 1)
                for b in range(NT):
                    ins = pe.transpose(BANK[4][:, 24 * b:24 * b + 24], GATE_ROWS[:, blk(b)], IDENT[0:24, 0:24])
                ins.then_inc(signal("gate_turned"), 1)

            pe_steps = {"gates": turn_gates, "sum": head_sum, "spread": head_spread, "rotate": head_rotate, "compress": compress}
            for what, j in IN2:
                if what == "out":
                    last = j
                elif what in pe_steps:
                    after.setdefault(last, []).append(lambda step=pe_steps[what], j=j: step(j))
            dense(lambda _: plan.steps["in2"], 0, operand(XH, XL),
                  token_major={LAST_V - 3 + b: b for b in range(NT)},
                  ready=lambda o, k, i: (signal("in2_x_lo"), k + 1, k), after=after)
            attention("nsa", (drained, plan.out0["merge"]), (signal("kc_done"), 1), (signal("gate_done"), NT),
                      (signal("head_done"), 6))
            pe.wait_ge(signal("ya_lo"), 4)

            def merge_operand(o, k):
                hi, lo = [(XH, XL), (XH, XL), (YAH, YAL), (YBH, YBL)][o % 4]
                return hi[:, k, :], lo[:, k, :]

            dense(lambda _: plan.steps["merge"], 0, merge_operand,
                  ready=lambda o, k, i: (signal("nsa_lo"), 2 * k + 2, k) if o % 4 == 3 else None)
            dense(lambda _: plan.steps["wo2"], 0, operand(MIXH, MIXL),
                  ready=lambda o, k, i: (signal("mix_lo"), k + 1, k))

            ffn = plan.steps["ffn_up"]
            per = 4 * KD

            def ffn_part(i):
                return ffn[i * per:(i + 1) * per]

            dense.n = FF2 // 2 + 1
            dense(ffn_part, 0, operand(XH, XL), ready=lambda o, k, i: (signal("norm2_x_lo"), k + 1, k),
                  after={0: [sums("norm2")], 1: [scales("norm2")]})
            with pe.Fori(1, FF2 // 2) as i:
                dense(ffn_part, i, operand(XH, XL))
            dense(lambda _: plan.steps["ffn_down"], 0, operand(H2H, H2L),
                  ready=lambda o, k, i: (signal("h2_lo"), k + 1, k))

        @block.scalar
        def _(act):
            act.dma_start(CT[:, 0:CONST_LATE], consts[:, 0:CONST_LATE]).then_inc(consts_in, 16)
            act.dma_start(GV[:], gains).then_inc(consts_in, 16)
            act.dma_start(POSB0[:], pos_rows[0]).then_inc(signal("pos_in"), 16)
            act.dma_start(POSI[:], pos_cols).then_inc(signal("pos_in"), 16)
            act.dma_start(MEM[:], mem).then_inc(mem_in, 16)
            act.dma_start(CT[:, CONST_LATE:], consts[:, CONST_LATE:]).then_inc(signal("late_consts_in"), 16)

            ahead = [0]

            def hi_part(tile_of, i, n_iter=NCH):
                slot = tile_of(i if isinstance(i, int) else 1) % RING
                act.wait_ge(raw_in[slot], over(lambda c: 16 * (tile_of(c) // RING + 1), i, n_iter))
                if not (isinstance(i, int) and tile_of(i) < RING):
                    act.wait_ge(products_done, over(lambda c: plan.tile_mark[tile_of(c) - RING], i, n_iter))
                act.activation(WH[:, slot, :], RAW[:, slot, :], ACT.Copy).then_inc(hi_done, 1)

            def keep_ahead(o, tiles=AHEAD):
                while ahead[0] <= min(plan.out_tile[o] + tiles, plan.tiles - 1):
                    n = ahead[0]
                    hi_part(lambda c: n, 0)
                    ahead[0] += 1

            def keep_ahead_in_loop(o, i, ref, per, n_iter):
                while ahead[0] <= plan.out_tile[o] + AHEAD:
                    n = ahead[0]
                    hi_part(lambda c: n + per * (c - ref), i, n_iter)
                    ahead[0] += 1

            def square(norm, m, src, tokens=S, scale=1.0):
                g = SQUARES0[norm] + m
                if g:
                    act.wait_ge(added, g)
                act.activation(SQ[:, 0:tokens], src, ACT.Square, scale=scale).then_inc(squared, 1)

            def std(norm, tokens=S):
                act.wait_ge(signal("var_done"), NORM_NO[norm] + 1)
                act.activation(STD[:, 0:tokens // P], VAR[:, 0:tokens // P], ACT.Sqrt).then_inc(std_done, 1)

            def x_hi(stage, norm_gain, m):
                act.activation(XH[:, m, :], X[:, m, :], ACT.Copy, scale=gain(norm_gain, m)
                               ).then_inc(signal(stage + "_x_hi"), 1)

            def attention(name):
                units, prob, pt = ATTENTION[name]
                n = len(units)
                for i in range(n + VALUE_LAG + 1):
                    j = i - TURN_LAG
                    if 0 <= j < n:
                        u = units[j]
                        act.wait_ge(signal(name + "_turned"), j + 1)
                        if j >= len(pt):
                            act.wait_ge(signal(name + "_values"), j - len(pt) + 1)
                        w, cols = min(P, u.nk), u.nb * P
                        act.activation(pt[j % len(pt)][0:w, 0:cols], BANK[TURNED[j % len(TURNED)]][0:w, 0:cols],
                                       ACT.Copy).then_inc(signal(name + "_pt"), 1)
                    if i < n:
                        u = units[i]
                        row, c = prob[i % len(prob)][:, u.terms], i % 8
                        act.wait_ge(signal(name + "_biased"), i + 1)
                        act.activation(row, row, ACT.Exp, scale=-1.0, bias=LEAST[:, c:c + 1],
                                       accum_out=SUM[:, c:c + 1]).then_inc(signal(name + "_exp"), 1)
                    j = i - VALUE_LAG - 1
                    if j >= 0 and units[j].head_end:
                        u = units[j]
                        act.wait_ge(signal(name + "_values"), j + 1)
                        act.activation(u.head_end[0], BANK[HEAD_OUT[u.head % 2]][0:HD, :], ACT.Copy
                                       ).then_inc(signal(name + "_hi"), 1)

            def output_projection(stage, norm, x_stage, own_operand=False):
                o0 = plan.out0[stage]
                for m in range(KD):
                    keep_ahead(o0 + m)
                    if m == KD - 1 and not own_operand:
                        act.wait_ge(products_done, plan.out_mark[o0 + KD - 1])
                        for j in range(KD // 2):
                            x_hi(x_stage, norm, j)
                    act.wait_ge(drained, o0 + m + 1)
                    square(norm, m, X[:, m, :])
                    if own_operand:
                        x_hi(x_stage, norm, m)
                if not own_operand:
                    for m in range(KD // 2, KD):
                        x_hi(x_stage, norm, m)

            def mlp(name, norm_after, gain_after, stage_after):
                o0, t0 = plan.out0[name], plan.tile0[name]

                def up(i, keep):
                    for m in range(CH + 1):
                        if m < CH:
                            out_of = lambda c: o0 + 16 * c + m
                            keep(m)
                            act.wait_ge(products_done, over(lambda c: plan.out_mark[out_of(c)], i))
                            act.wait_ge(drained, over(lambda c: out_of(c) - 1, i))
                            act.activation(TMP[:, m % 2, :], BANK[(o0 + m) % RING][:], ACT.Relu
                                           ).then_inc(signal(name + "_relu"), 1)
                            if m == 0 and isinstance(i, int) and i == 0:
                                std(name)
                        if m >= 1:
                            act.wait_ge(drained, over(lambda c: o0 + 16 * c + m, i))
                            act.activation(HH[:, m - 1, :], AB[:, (m - 1) % 2, :], ACT.Copy
                                           ).then_inc(signal(name + "_h_hi"), 1)

                def chunk(i):
                    up(i, lambda m: keep_ahead(o0 + 16 * i + m))
                    for m in range(KD):
                        keep_ahead(o0 + 16 * i + 8 + m)
                        if i == NCH - 1:
                            act.wait_ge(signal(name + "_x_added"), KD * (NCH - 1) + m + 1)
                            square(norm_after, m, X[:, m, :])
                            if stage_after:
                                x_hi(stage_after, gain_after, m)

                chunk(0)
                with act.Fori(1, NCH - 1) as i:
                    def keep(m):
                        keep_ahead_in_loop(o0 + 16 + m, i, 1, 16, NCH)
                    up(i, keep)
                    for m in range(KD):
                        keep(8 + m)
                ahead[0] += 16 * (NCH - 3)
                chunk(NCH - 1)

            in0, memo = plan.out0["in0"], plan.out0["mem"]
            act.wait_ge(consts_in, 32)
            for m in range(KD):
                if m % 2 == 0:
                    act.wait_ge(x_in[m // 2], 16)
                x_hi("in0", "attn0", m)
                if m == 0:
                    keep_ahead(in0, 0)
            for m in range(KD):
                square("in0", m, X[:, m, :])
                if 1 <= m < AHEAD:
                    keep_ahead(in0, m)
            keep_ahead(in0)
            std("in0")
            keep_ahead(in0 + 1)
            act.wait_ge(mem_in, 16)
            for m in range(KD):
                square("mem", m, MEM[:, m, :], NMEM)
                if m % 4 == 3:
                    keep_ahead(in0 + 2 + m // 4)
            std("mem", NMEM)
            keep_ahead(in0 + 4)
            for m in range(KD):
                act.wait_ge(signal("mem_scaled"), m + 1)
                act.activation(MH_[:, m, :], TMP[:, m % 2, 0:NMEM], ACT.Copy).then_inc(signal("mem_hi"), 1)
                if m % 4 == 3:
                    keep_ahead(in0 + 5 + m // 4)

            def c_squares(norm, first):
                for j in range(NORM_K[norm]):
                    square(norm, j, C32[:, first + j, :])

            def c_hi(first, n):
                for j in range(first, first + n):
                    act.wait_ge(signal("c_scaled"), j + 1)
                    act.activation(XH[:, j, :], TMP[:, j % 2, :], ACT.Copy).then_inc(signal("c_hi"), 1)

            act.wait_ge(drained, in0 + 2)
            c_squares("c_kv", 0)
            keep_ahead(in0 + 7)
            keep_ahead(memo)
            std("c_kv")
            keep_ahead(memo + 1)
            act.wait_ge(products_done, plan.out_mark[in0 + 7])
            c_hi(0, KKV)
            c_squares("c_q", KKV)
            keep_ahead(memo + 2)
            keep_ahead(memo + 3)
            std("c_q")
            keep_ahead(memo + 5)
            act.wait_ge(signal("angles0"), 2)
            act.activation(COS0[:], COS0[:], ACT.Sin).then_inc(signal("sines0"), 1)
            act.activation(SIN0[:], SIN0[:], ACT.Sin).then_inc(signal("sines0"), 1)
            keep_ahead(memo + 7)
            up0 = plan.out0["up0"]
            keep_ahead(up0)
            keep_ahead(up0 + 3)
            act.wait_ge(products_done, plan.out_mark[memo + 7])
            act.wait_ge(signal("key_ready"), 1)
            for h in range(NH):
                act.activation(KT0[HD:QK, h, :], KR[HD:QK, :], ACT.Copy).then_inc(signal("key_placed"), 1)
                keep_ahead(up0 + 3 + h // 2)
                if h == 3:
                    c_hi(KKV, KQ)
            for o in range(9, 14):
                keep_ahead(up0 + o)
            act.wait_ge(signal("c_lo"), KKV + KQ)
            for h in range(NH):
                keep_ahead(up0 + 14 + h)
                act.wait_ge(products_done, plan.out_mark[up0 + 14 + h])
                if h >= 2:
                    act.wait_ge(signal("q0_rotated"), h - 1)
                act.activation(TMP[0:QK, h % 2, :], BANK[(up0 + 14 + h) % RING][0:QK, :], ACT.Copy
                               ).then_inc(signal("q0_copied"), 1)
            attention("mla")
            output_projection("wo0", "mlp0", "mlp0")
            mlp("mlp0", "in1", "attn1", "in1")

            act.dma_start(POSB1[:], pos_rows[0]).then_inc(signal("pos1_in"), 16)
            in1 = plan.out0["in1"]
            keep_ahead(in1)
            std("in1")
            for o in range(14):
                keep_ahead(in1 + o)
            attention("swa")
            output_projection("wo1", "mlp1", "mlp1")
            act.wait_ge(signal("gains_done"), 1)
            mlp("mlp1", "final", "final_norm1", "in2")

            act.dma_start(POSB2, pos_rows[1]).then_inc(signal("pos2_in"), 16)
            act.dma_start(W1[:], cmp_w1).then_inc(signal("w_cmp_in"), 16)
            act.dma_start(W2[:], cmp_w2).then_inc(signal("w_cmp_in"), 16)
            in2 = plan.out0["in2"]
            keep_ahead(in2)
            std("final")
            for m in range(KD):
                square("norm1", m, X[:, m, :], scale=gain("final", m))
            keep_ahead(in2 + 2)
            std("norm1")

            def head_square(j):
                act.wait_ge(drained, in2 + j + 1)
                if j:
                    act.wait_ge(signal("head_sums"), j)
                else:
                    act.wait_ge(scale_done, NORM_NO["norm1"] + 1)
                act.activation(ACC[:], R32[:, j, :], ACT.Square).then_inc(signal("head_squares"), 1)

            for what, j in IN2:
                if what == "out":
                    keep_ahead(in2 + j)
                    if j == 6:
                        act.wait_ge(signal("angles2"), 2)
                        act.activation(COS2[:], COS2[:], ACT.Sin).then_inc(signal("sines2"), 1)
                        act.activation(SIN2[:], SIN2[:], ACT.Sin).then_inc(signal("sines2"), 1)
                    if j == CHANNELS + 3:
                        act.wait_ge(drained, in2 + GATES + 1)
                        act.activation(GATE_ROWS, GATE_ROWS, ACT.Sigmoid).then_inc(signal("gate_sigmoid"), 1)
                    if CHANNELS <= j < LAST_V and (j - CHANNELS) % 3 == 2:
                        m = (j - CHANNELS) // 3
                        act.wait_ge(signal("ya_done"), m + 1)
                        act.activation(YAH[:, m, :], PT2[:, m % 2, :], ACT.Copy).then_inc(signal("ya_hi"), 1)
                elif what == "sum":
                    head_square(j)
                elif what == "scale":
                    act.wait_ge(signal("head_var"), j + 1)
                    act.activation(HR[0:96, j, :], HR[0:96, j, :], ACT.Sqrt).then_inc(signal("head_std"), 1)
                elif what == "compress" and j == 1:
                    act.wait_ge(signal("cmp_bias"), 1)
                    for x_ in range(2):
                        act.activation(H1[:, x_, 0:2 * NCMP], BANK[4][0:HD, 64 * x_:64 * x_ + 2 * NCMP], ACT.Silu,
                                       bias=CB[0:HD, x_:x_ + 1]).then_inc(signal("cmp_silu"), 1)
                elif what == "compress" and j == 3:
                    act.wait_ge(signal("cmp_var"), 1)
                    act.activation(KC[:, 0:2 * NCMP], KC[:, 0:2 * NCMP], ACT.Sqrt).then_inc(signal("cmp_std"), 1)
            act.wait_ge(signal("ya_lo"), 4)
            attention("nsa")

            mo = plan.out0["merge"]
            for m in range(KD):
                for g in range(2):
                    keep_ahead(mo + 4 * m + g)
                    act.wait_ge(drained, mo + 4 * m + g + 1)
                    act.activation(TMP[:, g, :], TMP[:, g, :], ACT.Sigmoid).then_inc(signal("merge_gate"), 1)
                keep_ahead(mo + 4 * m + 3)
                act.wait_ge(signal("mix_done"), m + 1)
                act.activation(MIXH[:, m, :], TMP[:, 0, :], ACT.Copy).then_inc(signal("mix_hi"), 1)
            output_projection("wo2", "norm2", "norm2", own_operand=True)

            fo = plan.out0["ffn_up"]

            def ffn_body(i, keep, first=False):
                for j in range(2):
                    keep(2 * j)
                    if first and j == 0:
                        std("norm2")
                    act.wait_ge(signal("conv_done"), over(lambda c: 2 * c + j + 1, i, FF2 // 2 + 1))
                    b = GV[:, GAIN["ffn_b"] + j + 2 * i:GAIN["ffn_b"] + j + 2 * i + 1] if isinstance(i, int) else \
                        GV[:, bass.ds(i * 2 + (GAIN["ffn_b"] + j), 1)]
                    act.activation(TMP[:, 1, :], TMP[:, 0, :], ACT.Silu, bias=b).then_inc(signal("silu_done"), 1)
                    keep(2 * j + 1)
                    act.wait_ge(signal("h2_done"), over(lambda c: 2 * c + j + 1, i, FF2 // 2 + 1))
                    dst = H2H[:, 2 * i + j, :] if isinstance(i, int) else \
                        H2H[:, bass.ds(i * 2 + j, 1), :].rearrange("p a n -> p (a n)")
                    act.activation(dst, SQ[:], ACT.Copy).then_inc(signal("h2_hi"), 1)

            ffn_body(0, lambda q: keep_ahead(fo + q), first=True)
            with act.Fori(1, FF2 // 2) as i:
                ffn_body(i, lambda q: keep_ahead_in_loop(fo + 4 + q, i, 1, 4, FF2 // 2 + 1))
            ahead[0] += 4 * (FF2 // 2 - 2)
            for m in range(KD):
                keep_ahead(plan.out0["ffn_down"] + m)

        @block.vector
        def _(dve):
            own = Order(dve, signal("dve_own"))

            def add_square(norm, m, tokens=S):
                g = SQUARES0[norm] + m
                dve.wait_ge(squared, g + 1)
                if m == 0:
                    ins = dve.tensor_copy(ACC[:, 0:tokens], SQ[:, 0:tokens])
                else:
                    dve.wait_ge(added, g)
                    ins = dve.tensor_tensor(ACC[:, 0:tokens], ACC[:, 0:tokens], SQ[:, 0:tokens], ALU.add)
                ins.then_inc(added, 1)

            def scale_columns(norm, width, tokens=S, factor=1.0, diagonal=ACC, of_normed=False):
                n, nt = NORM_NO[norm], tokens // P
                dve.wait_ge(sums_done, n + 1)
                if of_normed:
                    own.then(dve.tensor_scalar(VAR[:, 0:nt], BANK[4][:, 0:nt], 1.0 / width, None, ALU.mult))
                    for _ in range(2):
                        own.then(dve.tensor_tensor(VAR[:, 0:nt], VAR[:, 0:nt], RCOL[:, 0:nt], ALU.mult))
                    dve.tensor_scalar(VAR[:, 0:nt], VAR[:, 0:nt], EPS, None, ALU.add).then_inc(signal("var_done"), 1)
                else:
                    dve.tensor_scalar(VAR[:, 0:nt], BANK[4][:, 0:nt], 1.0 / width, EPS, ALU.mult, ALU.add
                                      ).then_inc(signal("var_done"), 1)
                dve.wait_ge(std_done, n + 1)
                if of_normed:
                    own.then(dve.reciprocal(STD[:, 0:nt], STD[:, 0:nt]))
                    own.then(dve.tensor_tensor(RCOL[:, 0:nt], RCOL[:, 0:nt], STD[:, 0:nt], ALU.mult))
                else:
                    own.then(dve.reciprocal(RCOL[:, 0:nt], STD[:, 0:nt]))
                for t in range(nt):
                    ins = dve.tensor_scalar(diagonal[:, blk(t)], IDENT, RCOL[:, t:t + 1], factor, ALU.mult, ALU.mult)
                    if t < nt - 1:
                        own.step(ins)
                ins.then_inc(diag_done, 1)

            def scale_rows(norm, dst, tokens=S):
                n = NORM_NO[norm]
                dve.wait_ge(scale_done, n + 1)
                dve.tensor_copy(dst[:, 0:tokens], BANK[5][:, 0:tokens]).then_inc(scale_used, 1)
                dve.wait_ge(scale_used, n + 1)

            def x_lo(stage, norm_gain, m):
                dve.wait_ge(signal(stage + "_x_hi"), m + 1)
                dve.scalar_tensor_tensor(XL[:, m, :], X[:, m, :], gain(norm_gain, m), XH[:, m, :].bitcast(F32),
                                         ALU.mult, ALU.subtract).then_inc(signal(stage + "_x_lo"), 1)

            def output(o):
                dve.wait_ge(products_done, plan.out_mark[o])
                return BANK[o % RING]

            def both_halves(o, dst, j, by=None, factor=1.0):
                bank = output(o)
                for half in range(2):
                    rows = slice(HD * half, HD * half + HD)
                    if by is None:
                        ins = dve.tensor_copy(dst[:, 2 * j + half, :], bank[rows, 0:dst.shape[-1]])
                    else:
                        ins = dve.scalar_tensor_tensor(dst[:, 2 * j + half, :], bank[rows, :], factor, by[rows, :],
                                                       ALU.mult, ALU.mult)
                    if not half:
                        own.step(ins)
                ins.then_inc(drained, 1)

            def angles(pos, posf, inv, angle, turns, cos, sin, done):
                c1 = TWO_PI_PARTS
                own.then(dve.tensor_copy(posf, pos))
                own.then(dve.tensor_scalar(angle, posf, inv, None, ALU.mult))
                for dst, quarter in ((cos, 0.25), (sin, 0.0)):
                    own.then(dve.tensor_scalar(turns, angle, 1.0 / (2 * np.pi), quarter, ALU.mult, ALU.add))
                    own.then(dve.tensor_scalar(turns, turns, MAGIC, -MAGIC, ALU.add, ALU.add))
                    own.then(dve.scalar_tensor_tensor(dst, turns, -c1[0], angle, ALU.mult, ALU.add))
                    own.then(dve.scalar_tensor_tensor(dst, turns, -c1[1], dst, ALU.mult, ALU.add))
                    own.then(dve.scalar_tensor_tensor(dst, turns, -c1[2], dst, ALU.mult, ALU.add))
                    own.then(dve.tensor_scalar(dst, dst, 2 * np.pi * quarter, PI_MAX, ALU.add, ALU.min))
                    dve.tensor_scalar(dst, dst, -PI_MAX, None, ALU.max).then_inc(signal(done), 1)

            def attention(name):
                units, prob, pt = ATTENTION[name]
                n = len(units)
                for i in range(n + VALUE_LAG + 2):
                    if i < n:
                        u = units[i]
                        row = prob[i % len(prob)]
                        dve.wait_ge(signal(name + "_scores"), i + 1)
                        if i >= len(prob):
                            dve.wait_ge(signal(name + "_turned"), i - len(prob) + 1)
                        if name == "swa" and i < NH * NT and i % NT == 0:
                            dve.wait_ge(signal("bias_written"), 2 * (i // NT + 1))
                        dve.tensor_tensor_reduce(row[:, u.terms], BANK[SCORES[i % len(SCORES)]][:, u.terms], u.mask,
                                                 1.0, 3e38, ALU.add, ALU.min, LEAST[:, i % 8:i % 8 + 1]
                                                 ).then_inc(signal(name + "_biased"), 1)
                    if 2 <= i < n + 2:
                        u, c = units[i - 2], (i - 2) % 8
                        row = prob[(i - 2) % len(prob)][:, u.keys]
                        own.wait()
                        if u.weight is not None:
                            dve.tensor_scalar(row, row, RS[:, c:c + 1], u.weight, ALU.mult, ALU.mult
                                              ).then_inc(signal(name + "_prob"), 1)
                        else:
                            dve.tensor_scalar(row, row, RS[:, c:c + 1], None, ALU.mult
                                              ).then_inc(signal(name + "_prob"), 1)
                    if 1 <= i <= n:
                        c = (i - 1) % 8
                        dve.wait_ge(signal(name + "_exp"), i)
                        own.step(dve.reciprocal(RS[:, c:c + 1], SUM[:, c:c + 1]))
                    j = i - VALUE_LAG - 2
                    if j >= 0 and units[j].head_end:
                        u = units[j]
                        hi, lo = u.head_end
                        dve.wait_ge(signal(name + "_hi"), u.head + 1)
                        dve.tensor_tensor(lo, BANK[HEAD_OUT[u.head % 2]][0:HD, :], hi.bitcast(F32), ALU.subtract
                                          ).then_inc(signal(name + "_lo"), 1)

            def output_projection(stage, norm, x_stage, own_operand=False):
                o0 = plan.out0[stage]
                for m in range(KD + 1):
                    if m < KD:
                        bank = output(o0 + m)
                        dve.tensor_tensor(X[:, m, :], X[:, m, :], bank[:], ALU.add).then_inc(drained, 1)
                    if m == KD and not own_operand:
                        for j in range(KD // 2):
                            x_lo(x_stage, norm, j)
                    if m >= 1:
                        add_square(norm, m - 1)
                        if own_operand:
                            dve.wait_ge(drained, o0 + m)
                            x_lo(x_stage, norm, m - 1)
                if not own_operand:
                    dve.wait_ge(drained, o0 + KD)
                    for m in range(KD // 2, KD):
                        x_lo(x_stage, norm, m)

            def mlp(name, norm_after, gain_after, stage_after):
                o0 = plan.out0[name]

                def chunk(i):
                    static = isinstance(i, int)
                    for m in range(CH + 1):
                        if m < CH:
                            dve.wait_ge(signal(name + "_relu"), over(lambda c: CH * c + m + 1, i))
                            if not (static and i == 0 and m < 2):
                                dve.wait_ge(signal(name + "_h_lo"), over(lambda c: CH * c + m - 1, i))
                            dve.tensor_tensor(AB[:, m % 2, :], TMP[:, m % 2, :], TMP[:, m % 2, :], ALU.mult
                                              ).then_inc(drained, 1)
                        if static and i == 0 and m == 0:
                            scale_columns(name, D)
                        if static and i == 0 and m == 2:
                            scale_rows(name, RBC)
                            own.then(dve.tensor_tensor(RB2[:], RBC[:], RBC[:], ALU.mult))
                        if m >= 1:
                            dve.wait_ge(signal(name + "_h_hi"), over(lambda c: CH * c + m, i))
                            dve.tensor_tensor(HL[:, m - 1, :], AB[:, (m - 1) % 2, :], HH[:, m - 1, :].bitcast(F32),
                                              ALU.subtract).then_inc(signal(name + "_h_lo"), 1)
                    for m in range(KD + 1):
                        if m < KD:
                            out_of = lambda c: o0 + 16 * c + 8 + m
                            dve.wait_ge(products_done, over(lambda c: plan.out_mark[out_of(c)], i))
                            if not (static and i == 0 and m < 2):
                                dve.wait_ge(signal(name + "_x_added"), over(lambda c: KD * c + m - 1, i))
                            dve.tensor_tensor(DT[:, m % 2, :], BANK[(o0 + 8 + m) % RING][:], RB2[:], ALU.mult
                                              ).then_inc(drained, 1)
                            dve.wait_ge(drained, over(lambda c: out_of(c) + 1, i))
                            dve.tensor_tensor(X[:, m, :], X[:, m, :], DT[:, m % 2, :], ALU.add
                                              ).then_inc(signal(name + "_x_added"), 1)
                        if static and i == NCH - 1 and m >= 1:
                            add_square(norm_after, m - 1)
                            if stage_after:
                                x_lo(stage_after, gain_after, m - 1)

                chunk(0)
                with dve.Fori(1, NCH - 1) as i:
                    chunk(i)
                chunk(NCH - 1)

            in0, memo = plan.out0["in0"], plan.out0["mem"]
            dve.wait_ge(consts_in, 32)
            for m in range(KD):
                if m % 2 == 0:
                    dve.wait_ge(x_in[m // 2], 16)
                x_lo("in0", "attn0", m)
            for m in range(KD):
                add_square("in0", m)
            scale_columns("in0", D, diagonal=TMP[:, 0, :])
            for m in range(KD):
                add_square("mem", m, NMEM)
            scale_rows("in0", RBC)

            def c_out(j):
                dve.tensor_tensor(C32[:, j, :], output(in0 + j)[:], RBC[:], ALU.mult).then_inc(drained, 1)

            for j in range(3):
                c_out(j)
            scale_columns("mem", D, NMEM)
            c_out(3)
            scale_rows("mem", ACC, NMEM)
            for m in range(KD + 1):
                if m < KD:
                    if m >= 2:
                        dve.wait_ge(signal("mem_lo"), m - 1)
                    dve.scalar_tensor_tensor(TMP[:, m % 2, 0:NMEM], MEM[:, m, :], gain("mem", m), ACC[:, 0:NMEM],
                                             ALU.mult, ALU.mult).then_inc(signal("mem_scaled"), 1)
                if m >= 1:
                    dve.wait_ge(signal("mem_hi"), m)
                    dve.wait_ge(signal("mem_scaled"), m)
                    dve.tensor_tensor(ML_[:, m - 1, :], TMP[:, (m - 1) % 2, 0:NMEM], MH_[:, m - 1, :].bitcast(F32),
                                      ALU.subtract).then_inc(signal("mem_lo"), 1)
                if m == 4:
                    c_out(4)
            add_square("c_kv", 0)
            add_square("c_kv", 1)
            dve.tensor_tensor(KR[HD:QK, :], output(in0 + 5)[HD:QK, :], RBC[HD:QK, :], ALU.mult).then_inc(drained, 1)
            both_halves(in0 + 6, QX, 0, RBC, -SCALE)
            both_halves(in0 + 7, QX, 1, RBC, -SCALE)

            def c_scale(norm, first):
                n = NORM_K[norm]
                for j in range(first, first + n + 1):
                    if j < first + n:
                        if j >= 2:
                            dve.wait_ge(signal("c_lo"), j - 1)
                        dve.scalar_tensor_tensor(TMP[:, j % 2, :], C32[:, j, :], gain(norm, j - first), ACC[:],
                                                 ALU.mult, ALU.mult).then_inc(signal("c_scaled"), 1)
                    if j > first:
                        dve.wait_ge(signal("c_hi"), j)
                        dve.wait_ge(signal("c_scaled"), j)
                        dve.tensor_tensor(XL[:, j - 1, :], TMP[:, (j - 1) % 2, :], XH[:, j - 1, :].bitcast(F32),
                                          ALU.subtract).then_inc(signal("c_lo"), 1)

            def mem_out(o):
                l, q = o // 4, o % 4
                if q < 2:
                    both_halves(memo + o, KM[:, l, :, :], q)
                else:
                    dve.tensor_copy(VM[:, l, q - 2, :], output(memo + o)[:, 0:MH * HD]).then_inc(drained, 1)

            scale_columns("c_kv", P * KKV)
            mem_out(0)
            scale_rows("c_kv", ACC)
            c_scale("c_kv", 0)
            for j in range(KQ):
                add_square("c_q", j)
            mem_out(1)
            mem_out(2)
            scale_columns("c_q", P * KQ, factor=-MLA_SCALE)
            mem_out(3)
            dve.wait_ge(signal("pos_in"), 32)
            angles(POSB0[:], POSF0[:], const("inv_mla"), ANG0[:, 0, :], ANG0[:, 1, :], COS0[:], SIN0[:], "angles0")
            for o in range(4, 6):
                mem_out(o)
            scale_rows("c_q", ACC)

            dve.wait_ge(signal("sines0"), 2)
            own.step(dve.memset(COS0[0:HD, :], 1.0))
            own.then(dve.memset(SIN0[0:HD, :], 0.0))
            dve.wait_ge(signal("key_rotated"), 1)
            own.then(dve.tensor_tensor(KR[HD:QK, :], KR[HD:QK, :], COS0[HD:QK, :], ALU.mult))
            own.then(dve.tensor_tensor(TMP[HD:QK, 0, :], BANK[6][HD:QK, :], SIN0[HD:QK, :], ALU.mult))
            dve.tensor_tensor(KR[HD:QK, :], KR[HD:QK, :], TMP[HD:QK, 0, :], ALU.add).then_inc(signal("key_ready"), 1)
            dve.wait_ge(signal("key_ready"), 1)

            for o in range(6, 8):
                mem_out(o)
            up0 = plan.out0["up0"]
            for m in range(6):
                both_halves(up0 + m, KT0[0:HD, :, :], m)
            for b in range(NT):
                dve.tensor_copy(V0[:, b, S:NH * HD], output(up0 + 6 + b)[:, 0:NH * HD - S]).then_inc(drained, 1)
            c_scale("c_q", KKV)
            for b in range(NT):
                dve.tensor_copy(V0[:, b, 0:S], output(up0 + 10 + b)[:]).then_inc(drained, 1)
            dve.wait_ge(signal("key_placed"), NH)
            for h in range(NH + 1):
                if h < NH:
                    dve.wait_ge(signal("q0_copied"), h + 1)
                    dve.tensor_tensor(QT0[:, h, :], BANK[(up0 + 14 + h) % RING][0:QK, :], COS0[0:QK, :], ALU.mult
                                      ).then_inc(drained, 1)
                if h >= 1:
                    dve.wait_ge(signal("q0_rotated"), h)
                    if h >= 2:
                        dve.wait_ge(signal("q0_done"), h - 1)
                    dve.tensor_tensor(SQ[0:QK, :], BANK[6 + (h - 1) % 2][0:QK, :], SIN0[0:QK, :], ALU.mult
                                      ).then_inc(signal("q0_rotated_read"), 1)
                    dve.wait_ge(signal("q0_rotated_read"), h)
                    dve.wait_ge(drained, up0 + 14 + h)
                    dve.tensor_tensor(QT0[:, h - 1, :], QT0[:, h - 1, :], SQ[0:QK, :], ALU.add
                                      ).then_inc(signal("q0_done"), 1)
            dve.wait_ge(signal("late_consts_in"), 16)
            dve.wait_ge(signal("q0_done"), NH)
            attention("mla")
            output_projection("wo0", "mlp0", "mlp0")
            mlp("mlp0", "in1", "attn1", "in1")

            in1 = plan.out0["in1"]
            scale_columns("in1", D)
            scale_rows("in1", RBC)
            for m in range(2):
                both_halves(in1 + m, K1, m, RBC)
            for b in range(NT):
                dve.tensor_scalar(V1[:, b, :], output(in1 + 2 + b)[:, 0:NKV * HD], RCOL[:, b:b + 1], None, ALU.mult
                                  ).then_inc(drained, 1)
            dve.wait_ge(signal("pos1_in"), 16)
            own.step(dve.tensor_copy(POSQ, POSI[:, 0, :]))
            own.step(dve.tensor_scalar(SINK, GV[:, GAIN["sinks"]:GAIN["sinks"] + NH], -1.0, None, ALU.mult))
            own.then(dve.tensor_copy(POSF1[:], POSB1[:]))
            own.step(dve.memset(DIST[:, 0, 0:P], 0.0))
            for b in range(NT):
                lo_, k0 = (P, 0) if b == 0 else (0, (b - 1) * P)
                own.step(dve.tensor_scalar(DIST[:, b, lo_:2 * P], POSF1[:, k0:k0 + 2 * P - lo_], -1.0,
                                           POSQ[:, b:b + 1], ALU.mult, ALU.add))
            own.wait()
            for b in range(NT):
                lo_ = P if b == 0 else 0
                ins = dve.tensor_tensor(DIST[:, b, lo_:2 * P], DIST[:, b, lo_:2 * P], const("band", lo_, 2 * P - lo_),
                                        ALU.add)
                if b < NT - 1:
                    own.step(ins)
            ins.then_inc(signal("dist_done"), 1)
            for m in range(6):
                both_halves(in1 + 6 + m, Q1, m, RBC, -SCALE)
            for m in range(2):
                both_halves(in1 + 12 + m, QX, m, RBC, -SCALE)
            dve.wait_ge(drained, in1 + 14)
            for b in SCORES:
                dve.memset(BANK[b][:, 2 * P:2 * P + 1], 0.0).then_inc(signal("column_zeroed"), 1)
            dve.wait_ge(signal("column_zeroed"), len(SCORES))
            attention("swa")
            output_projection("wo1", "mlp1", "mlp1")
            dve.tensor_tensor(GF[:], GV[:, GAIN["final"]:GAIN["final"] + KD], GV[:, GAIN["norm1"]:GAIN["norm1"] + KD],
                              ALU.mult).then_inc(signal("gains_done"), 1)
            dve.wait_ge(signal("gains_done"), 1)
            mlp("mlp1", "final", "final_norm1", "in2")

            scale_columns("final", D, diagonal=TMP[:, 0, :])
            for m in range(KD):
                add_square("norm1", m)
            scale_rows("final", TMP[:, 1, :])
            scale_columns("norm1", D, of_normed=True)
            dve.wait_ge(signal("w_cmp_in"), 32)
            for x_, name in enumerate(("pe_k", "pe_v")):
                weighted = PROB2[:].rearrange("p a (j h) -> p (a j) h", h=HD)
                embedding = GV[:, GAIN[name]:GAIN[name] + 16].unsqueeze(2).to_broadcast([P, 16, HD])
                own.then(dve.tensor_tensor(weighted, W1[:, x_, :, :], embedding, ALU.mult))
                dve.tensor_reduce(PEW[:, x_, :], weighted.rearrange("p j h -> p h j"), AXX, ALU.add
                                  ).then_inc(signal("positions_weighted"), 1)
                dve.wait_ge(signal("positions_weighted"), x_ + 1)
            scale_rows("norm1", RBC)
            own.step(dve.memset(UP[:, 0:2], 0.0))
            own.step(dve.tensor_scalar(gain("q"), gain("q"), -SCALE, None, ALU.mult))
            in2 = plan.out0["in2"]

            def in2_out(o):
                if o == LAST_V:
                    for b in range(NT):
                        dve.tensor_scalar(VN[:, b, :], output(in2 + LAST_V - 3 + b)[:, 0:2 * P], RCOL[:, b:b + 1], None,
                                          ALU.mult).then_inc(drained, 1)
                    return
                bank = output(in2 + o)
                if o in (6, 7):
                    for g in range(NG):
                        rows = slice(HD * g, HD * g + HD)
                        own.step(dve.tensor_tensor(KCS[0:HD, o - 6, g, :], bank[rows, :], RBC[rows, :], ALU.mult))
                        ins = dve.tensor_tensor(KCS[HD:P, o - 6, g, 0:S - 1], bank[rows, 1:S], RBC[rows, 1:S], ALU.mult)
                        if g == 0:
                            own.step(ins)
                    ins.then_inc(drained, 1)
                elif o < 6:
                    dve.tensor_tensor(R32[:, o, :], bank[:], RBC[:], ALU.mult).then_inc(drained, 1)
                elif o == GATES:
                    dve.tensor_tensor(GATE_ROWS, bank[0:24, :], RBC[0:24, :], ALU.mult).then_inc(drained, 1)
                else:
                    m, q = (o - CHANNELS) // 3, (o - CHANNELS) % 3
                    if m and q == 0:
                        dve.wait_ge(signal("ya_done"), m)
                    dve.tensor_tensor(PROB2[:, (0, 1, 1)[q], :], bank[:], RBC[:], ALU.mult).then_inc(drained, 1)
                    if q == 1:
                        dve.wait_ge(drained, in2 + o + 1)
                        own.then(dve.tensor_tensor(UP[:, 2:S + 2], PROB2[:, 0, :], PROB2[:, 1, :], ALU.mult))
                        convolve(PROB2[:, 0, :], UP, lambda t: gain("conv_a", 3 * m + t))
                    elif q == 2:
                        dve.wait_ge(drained, in2 + o + 1)
                        if m >= 2:
                            dve.wait_ge(signal("ya_lo"), m - 1)
                        dve.tensor_tensor(PT2[:, m % 2, :], PROB2[:, 0, :], PROB2[:, 1, :], ALU.mult
                                          ).then_inc(signal("ya_done"), 1)
                        dve.wait_ge(signal("ya_hi"), m + 1)
                        dve.tensor_tensor(YAL[:, m, :], PT2[:, m % 2, :], YAH[:, m, :].bitcast(F32), ALU.subtract
                                          ).then_inc(signal("ya_lo"), 1)

            def convolve(dst, src, tap, done=None):
                own.then(dve.tensor_scalar(dst, src[:, 0:S], tap(0), None, ALU.mult))
                own.then(dve.scalar_tensor_tensor(dst, src[:, 1:S + 1], tap(1), dst, ALU.mult, ALU.add))
                ins = dve.scalar_tensor_tensor(dst, src[:, 2:S + 2], tap(2), dst, ALU.mult, ALU.add)
                if done:
                    ins.then_inc(done, 1)
                else:
                    own.then(ins)

            def head_scale(g):
                dve.wait_ge(signal("head_sums"), 3 * g + 3)
                dve.tensor_scalar(HR[0:96, g, :], BANK[6 - g][0:96, :], 1.0 / HD, EPS, ALU.mult, ALU.add
                                  ).then_inc(signal("head_var"), 1)
                dve.wait_ge(signal("head_std"), g + 1)
                dve.reciprocal(HR[0:96, g, :], HR[0:96, g, :]).then_inc(signal("head_scales"), 1)

            def head_norm(j):
                dve.wait_ge(signal("head_spread"), j + 1)
                if j >= 2:
                    dve.wait_ge(signal("head_done"), j - 1)
                dve.scalar_tensor_tensor(TMP[:, j % 2, :], R32[:, j, :], gain(("k_sel", "k_win", "q")[min(j, 2)]),
                                         BANK[6][:], ALU.mult, ALU.mult).then_inc(signal("head_normed"), 1)

            def head_rotated(j):
                if j == 0:
                    dve.wait_ge(signal("sines2"), 2)
                else:
                    dve.wait_ge(signal("head_done"), j)
                dve.wait_ge(signal("head_rotated"), j + 1)
                dve.tensor_tensor(SQ[:], BANK[7][:], SIN2[:], ALU.mult).then_inc(signal("head_rotated_read"), 1)
                dve.wait_ge(signal("head_normed"), j + 1)
                own.then(dve.tensor_tensor(R32[:, j, :], TMP[:, j % 2, :], COS2[:], ALU.mult))
                dve.wait_ge(signal("head_rotated_read"), j + 1)
                for half in range(2):
                    rows = slice(HD * half, HD * half + HD)
                    dst = KN[:, j, half, :] if j < 2 else QN[:, 2 * (j - 2) + half, :]
                    ins = dve.tensor_tensor(dst, R32[rows, j, :], SQ[rows, :], ALU.add)
                    if not half:
                        own.step(ins)
                ins.then_inc(signal("head_done"), 1)

            def compress(step):
                w = 2 * NCMP
                if step == 1:
                    dve.wait_ge(signal("cmp_hidden"), 1)
                    dve.tensor_copy(CB[0:HD, :], BANK[4][0:HD, 128:130]).then_inc(signal("cmp_bias"), 1)
                elif step == 2:
                    dve.wait_ge(signal("cmp_out"), 1)
                    own.step(dve.tensor_copy(VC[0:NCMP, :], BANK[4][0:NCMP, 320:448]))
                    own.then(dve.tensor_copy(KCT[:, 0, 0:w], BANK[4][0:HD, 256:256 + w]))
                    dve.tensor_tensor(KCT[:, 1, 0:w], KCT[:, 0, 0:w], KCT[:, 0, 0:w], ALU.mult
                                      ).then_inc(signal("cmp_squares"), 1)
                else:
                    dve.wait_ge(signal("cmp_sums"), 1)
                    dve.tensor_scalar(KC[:, 0:w], BANK[4][0:HD, 128:128 + w], 1.0 / HD, EPS, ALU.mult, ALU.add
                                      ).then_inc(signal("cmp_var"), 1)
                    dve.wait_ge(signal("cmp_std"), 1)
                    own.then(dve.reciprocal(KC[:, 0:w], KC[:, 0:w]))
                    dve.scalar_tensor_tensor(KC[:, 0:w], KCT[:, 0, 0:w], gain("k_cmp")[0:HD, :], KC[:, 0:w],
                                             ALU.mult, ALU.mult).then_inc(signal("kc_done"), 1)

            def gates(_):
                dve.wait_ge(signal("gate_turned"), 1)
                own.then(dve.tensor_copy(GATE[:].rearrange("p b n -> p (b n)"), BANK[4][:, 0:NT * 24]))
                for b in range(NT):
                    dve.tensor_scalar(GATE[:, b, 0:24:3], GATE[:, b, 0:24:3], const("cmp_valid", b), None, ALU.mult
                                      ).then_inc(signal("gate_done"), 1)

            for what, j in IN2:
                if what != "sum":
                    {"out": in2_out, "scale": head_scale, "spread": head_norm, "rotate": head_rotated,
                     "compress": compress, "gates": gates}[what](j)
                if what == "out" and j == 3:
                    for m in range(KD):
                        dve.scalar_tensor_tensor(X[:, m, :], X[:, m, :], gain("final", m), TMP[:, 1, :],
                                                 ALU.mult, ALU.mult).then_inc(signal("x_normed"), 1)
                    dve.wait_ge(signal("pos2_in"), 16)
                    angles(POSB2, POSF2, const("inv_nsa"), PROB2[:, 0, :], PROB2[:, 1, :], COS2[:], SIN2[:],
                           "angles2")
            dve.wait_ge(signal("gate_done"), NT)
            dve.wait_ge(signal("x_normed"), KD)
            dve.wait_ge(signal("ya_done"), 4)
            attention("nsa")

            mo = plan.out0["merge"]
            for m in range(KD):
                if m:
                    dve.wait_ge(signal("mix_lo"), m)
                for g in range(2):
                    dve.tensor_tensor(TMP[:, g, :], output(mo + 4 * m + g)[:], RBC[:], ALU.mult).then_inc(drained, 1)
                for g in range(2):
                    bank = output(mo + 4 * m + 2 + g)
                    dve.wait_ge(signal("merge_gate"), 2 * m + g + 1)
                    dve.tensor_tensor(TMP[:, g, :], TMP[:, g, :], bank[:], ALU.mult).then_inc(drained, 1)
                dve.wait_ge(drained, mo + 4 * m + 4)
                dve.tensor_tensor(TMP[:, 0, :], TMP[:, 0, :], TMP[:, 1, :], ALU.add).then_inc(signal("mix_done"), 1)
                dve.wait_ge(signal("mix_hi"), m + 1)
                dve.tensor_tensor(MIXL[:, m, :], TMP[:, 0, :], MIXH[:, m, :].bitcast(F32), ALU.subtract
                                  ).then_inc(signal("mix_lo"), 1)
            output_projection("wo2", "norm2", "norm2", own_operand=True)

            fo = plan.out0["ffn_up"]
            own.step(dve.memset(GB[:, :, 0:2], 0.0))

            def ffn_body(i, first=False):
                n_iter = FF2 // 2 + 1
                for j in range(2):
                    def out_of(c, up):
                        return fo + 4 * c + 2 * j + up

                    def tap(t):
                        at = GAIN["ffn_conv"] + 3 * j + t
                        return GV[:, at:at + 1] if isinstance(i, int) else GV[:, bass.ds(i * 6 + at, 1)]

                    if first and j == 0:
                        scale_columns("norm2", D)
                        scale_rows("norm2", RBC)
                    dve.wait_ge(products_done, over(lambda c: plan.out_mark[out_of(c, 0)], i, n_iter))
                    dve.tensor_tensor(GB[:, j, 2:S + 2], BANK[(fo + 2 * j) % RING][:], RBC[:], ALU.mult
                                      ).then_inc(drained, 1)
                    dve.wait_ge(drained, over(lambda c: out_of(c, 0) + 1, i, n_iter))
                    convolve(TMP[:, 0, :], GB[:, j, :], tap, signal("conv_done"))
                    dve.wait_ge(products_done, over(lambda c: plan.out_mark[out_of(c, 1)], i, n_iter))
                    if not (isinstance(i, int) and i == 0 and j == 0):
                        dve.wait_ge(signal("h2_lo"), over(lambda c: 2 * c + j, i, n_iter))
                    dve.tensor_tensor(SQ[:], BANK[(fo + 2 * j + 1) % RING][:], RBC[:], ALU.mult).then_inc(drained, 1)
                    dve.wait_ge(drained, over(lambda c: out_of(c, 1) + 1, i, n_iter))
                    dve.wait_ge(signal("silu_done"), over(lambda c: 2 * c + j + 1, i, n_iter))
                    dve.tensor_tensor(SQ[:], SQ[:], TMP[:, 1, :], ALU.mult).then_inc(signal("h2_done"), 1)
                    dve.wait_ge(signal("h2_hi"), over(lambda c: 2 * c + j + 1, i, n_iter))
                    if isinstance(i, int):
                        hi, lo = H2H[:, 2 * i + j, :], H2L[:, 2 * i + j, :]
                    else:
                        hi, lo = (t[:, bass.ds(i * 2 + j, 1), :].rearrange("p a n -> p (a n)") for t in (H2H, H2L))
                    dve.tensor_tensor(lo, SQ[:], hi.bitcast(F32), ALU.subtract).then_inc(signal("h2_lo"), 1)

            own.wait()
            ffn_body(0, first=True)
            start = own.n
            with dve.Fori(1, FF2 // 2) as i:
                own.more = i * 4 - 4
                ffn_body(i)
            assert own.n - start == 4
            own.more, own.n = 0, start + 4 * (FF2 // 2 - 1)
            for m in range(KD):
                bank = output(plan.out0["ffn_down"] + m)
                dve.tensor_tensor(X[:, m, :], X[:, m, :], bank[:], ALU.add).then_inc(drained, 1)


def units(w, n_k, width=P):
    n = w.shape[1] // width
    return w.reshape(n_k, P, n, width).transpose(2, 0, 1, 3).reshape(n * n_k, P, width)


def tiles(blocks, per_tile):
    n, _, width = blocks.shape
    count = -(-n // per_tile)
    out = np.zeros((count, P, TW), np.float32)
    for b in range(n):
        at = b % per_tile * width
        out[b // per_tile, :, at:at + width] = blocks[b]
    return out


def weight_stream(a):
    mla_in = a["mla_w_in"][0]
    q_rank, kv_rank = KQ * P, KKV * P
    key_rope = np.zeros((D, P), np.float32)
    key_rope[:, HD:QK] = mla_in[:, q_rank + kv_rank:q_rank + kv_rank + ROPE]
    out = [tiles(units(w, KD), UPT) for w in (
        mla_in[:, q_rank:q_rank + kv_rank], mla_in[:, :q_rank], key_rope, mla_in[:, q_rank + kv_rank + ROPE:])]
    for l in range(2):
        w = a["w_mem_kv"][l]
        out += [tiles(units(w[:, :MH * HD], KD), UPT), tiles(units(w[:, MH * HD:], KD, 2 * P), 4)]
    ukv = a["mla_w_ukv"][0].reshape(kv_rank, NH, 2 * HD)
    key, value = (np.ascontiguousarray(ukv[:, :, s]).reshape(kv_rank, NH * HD) for s in (slice(0, HD), slice(HD, 2 * HD)))
    k_units = units(key, KKV)
    second = np.concatenate([tiles(k_units[8:], 4)[0][:, :4 * P], tiles(units(value[:, S:], KKV, 256), 2)[0][:, :4 * P]], axis=1)
    out += [tiles(k_units[:8], UPT), second[None], tiles(units(value[:, :S], KKV, S), 2),
            tiles(units(a["mla_w_uq"][0], KQ, QK), 3 * KQ)]

    def mlp(l):
        for c in range(NCH):
            hidden = slice(c * CH * P, (c + 1) * CH * P)
            yield tiles(units(a["mlp_w_up"][l][:, hidden], KD), UPT)
            yield tiles(units(a["mlp_w_down"][l][hidden], CH), UPT)

    out += [tiles(units(a["w_o"][0], KD), UPT), *mlp(0)]
    w = a["swa_w_in"][0]
    nq, nk = NH * HD, NKV * HD
    out += [tiles(units(w[:, nq:nq + nk], KD), UPT), tiles(units(w[:, nq + nk:nq + 2 * nk], KD, 2 * P), 4),
            tiles(units(w[:, :nq], KD), UPT), tiles(units(w[:, nq + 2 * nk:], KD), UPT)]
    out += [tiles(units(a["w_o"][1], KD), UPT), *mlp(1)]
    w = a["w_in_2"][0]
    a_b, a_c, a_x, q, kc, vc, ksl, vsl, kwn, vwn, g_nsa, g_merge = np.split(
        w, np.cumsum([512, 512, 512, 512] + [P] * 6 + [24]), axis=1)
    out += [tiles(units(v, KD), UPT) for v in (ksl, kwn, q, kc, vc)] + [tiles(units(g_nsa, KD, 24), KD)]
    for m in range(4):
        out += [tiles(units(v[:, m * P:(m + 1) * P], KD), UPT) for v in (a_c, a_x, a_b)]
    out += [tiles(units(np.concatenate([vsl, vwn], axis=1), KD, 2 * P), 4)]
    for m in range(KD):
        c = slice(m * P, (m + 1) * P)
        out += [tiles(units(g_merge[:, :D][:, c], KD), UPT), tiles(units(g_merge[:, D:][:, c], KD), UPT),
                tiles(np.concatenate([units(a["w_a_out_2"][0][:, c], 4), units(a["w_b_out_2"][0][:, c], 4)]), UPT)]
    out += [tiles(units(a["w_o_2"][0], KD), UPT)]
    w = a["w_ffn_in_2"][0]
    for m in range(FF2):
        for half in range(2):
            at = (half * FF2 + m) * P
            out += [tiles(units(w[:, at:at + P], KD), UPT)]
    for m in range(KD):
        out += [tiles(units(a["w_ffn_out_2"][0][:, m * P:(m + 1) * P], FF2), UPT)]
    stream = np.concatenate(out)
    assert stream.shape[0] == PLAN.tiles, (stream.shape, PLAN.tiles)
    return stream


def gain_columns(a):
    def cols(v):
        return v.reshape(-1, P).T

    def heads(v):
        return np.concatenate([v, v])[:, None]

    out = {"attn0": cols(a["attn_norm_g"][0]), "attn1": cols(a["attn_norm_g"][1]),
           "mlp0": cols(a["mlp_norm_g"][0]), "mlp1": cols(a["mlp_norm_g"][1]), "mem": cols(a["mem_norm_g"]),
           "final": cols(a["final_norm_g"]), "c_kv": cols(a["mla_kv_norm_g"][0]), "c_q": cols(a["mla_q_norm_g"][0]),
           "norm1": cols(a["norm1_g_2"][0]), "norm2": cols(a["norm2_g_2"][0]), "q": heads(a["q_norm_g_2"][0]),
           "k_cmp": heads(a["k_norm_g_2"][0, 0]), "k_sel": heads(a["k_norm_g_2"][0, 1]),
           "k_win": heads(a["k_norm_g_2"][0, 2]),
           "conv_a": a["conv_a_w_2"][0].reshape(3, 4, P).transpose(2, 1, 0).reshape(P, 12),
           "ffn_conv": a["ffn_conv_w_2"][0].reshape(3, FF2, P).transpose(2, 1, 0).reshape(P, 3 * FF2),
           "ffn_b": cols(a["ffn_conv_b_2"][0]), "sinks": np.broadcast_to(a["swa_sinks"][0][None], (P, NH)),
           "pe_k": cols(a["cmp_k_pe_2"][0].reshape(-1)), "pe_v": cols(a["cmp_v_pe_2"][0].reshape(-1))}
    return np.ascontiguousarray(np.concatenate([out[name] for name in GAIN], axis=1))


def constants():
    p, c = np.arange(P)[:, None], np.arange(P)[None, :]

    def rotation(first, half, n):
        r = np.zeros((P, P), np.float32)
        for run in range(first, first + n * 2 * half, 2 * half):
            for d in range(half):
                r[run + half + d, run + d] = -1.0
                r[run + d, run + half + d] = 1.0
        return r

    def inverse_frequencies(half, at):
        f = np.float32(10000.0) ** (-(np.arange(half, dtype=np.float32) * np.float32(2.0)) / np.float32(2 * half))
        return np.where(at >= 0, f.astype(np.float32)[at % half], 0).astype(np.float32)[:, None]

    rows = np.arange(P)
    end = np.arange(32) * (CMP // 2) + CMP - 1
    t = np.arange(S).reshape(NT, P).T
    cmp_mask = np.where((end[None, None, :] <= t[:, :, None]) & (np.arange(32) < NCMP)[None, None, :], 0, MASKED)
    out = {
        "tri": np.concatenate([np.zeros((P, S - P)), np.where(c <= p, 0, MASKED)], axis=1),
        "ident": np.eye(P), "ones": np.ones((P, P)), "rot96": rotation(HD, ROPE // 2, 1),
        "head_rows": p // HD == c[:, 0:32], "head_spread": p % 32 == c // HD, "rot128": rotation(0, HD // 2, 2),
        "band": np.concatenate([np.where(c > p, 0, MASKED), np.where(c <= p, 0, MASKED)], axis=1),
        "cmp_mask": cmp_mask.reshape(P, NT * 32), "cmp_valid": t >= CMP - 1,
        "slopes": np.broadcast_to(2.0 ** (-8.0 * (np.arange(NH) + 1.0) / NH), (P, NH)),
        "inv_mla": inverse_frequencies(ROPE // 2, np.where((rows >= HD) & (rows < QK), (rows - HD) % (ROPE // 2), -1)),
        "inv_nsa": inverse_frequencies(HD // 2, rows % (HD // 2))}
    return np.ascontiguousarray(np.concatenate([out[name].astype(np.float32) for name in CONST], axis=1))


def kernel(**inputs):
    import concourse.bacc as bacc
    from concourse.bass_utils import run_bass_kernel_spmd

    a = {name: np.asarray(v) for name, v in inputs.items()}

    def feature_major(v):
        return np.ascontiguousarray(v[0].T.reshape(KD, P, -1).transpose(1, 0, 2))

    positions = np.stack([a["positions"][0], a["positions_2"][0]])
    arrays = {
        "stream": weight_stream(a), "gains": gain_columns(a), "consts": constants(),
        "x": feature_major(a["x"]), "mem": feature_major(a["mem"]),
        "pos_rows": np.ascontiguousarray(np.broadcast_to(positions[:, None, :], (2, P, S))),
        "pos_cols": np.ascontiguousarray(positions.reshape(2, NT, P).transpose(2, 0, 1)),
        "cmp_w1": np.ascontiguousarray(np.stack(
            [a[n][0].reshape(16, P, HD).transpose(1, 0, 2) for n in ("cmp_k_w1_2", "cmp_v_w1_2")], axis=1)),
        "cmp_w2": np.ascontiguousarray(np.stack([a[n][0] for n in ("cmp_k_w2_2", "cmp_v_w2_2")], axis=1))}
    nc = bacc.Bacc("TRN2", target_bir_lowering=False, num_devices=1)
    args = [nc.dram_tensor(name, v.shape, mybir.dt.from_np(v.dtype), kind="ExternalInput").ap()
            for name, v in arrays.items()]
    out = nc.dram_tensor("out", (P, KD, S), F32, kind="ExternalOutput").ap()
    program(nc, *args, out)
    r = run_bass_kernel_spmd(nc, [arrays], core_ids=[0])
    got = np.asarray(r.results[0]["out"])
    return np.ascontiguousarray(got.transpose(1, 0, 2).reshape(D, S).T)[None]
```
